# Optimizing a Trainium2 kernel written in Bass

```python
import jax, jax.numpy as jnp
from jax import lax
import numpy as np

D_MODEL = 1024
BATCH = 1
SEQ = 256
DEPTH = 2

GRID_W = 64
CTX_LEN = 256
HEAD_DIM = 64
ATTN_WIDTH = D_MODEL // 2
N_Q_HEADS = ATTN_WIDTH // HEAD_DIM
N_KV_HEADS = 2
Q_GROUP = N_Q_HEADS // N_KV_HEADS
KV_WIDTH = N_KV_HEADS * HEAD_DIM
ATTN_SCALE = HEAD_DIM ** -0.5
Q_BLOCK = 128
ROPE_THETA = 10000.0
POOL_WINDOWS = (2, 4, 8, 16)
POOL_WIDTH = D_MODEL - ATTN_WIDTH
POOL_GROUP_DIM = POOL_WIDTH // len(POOL_WINDOWS)
IN_A_WIDTH = ATTN_WIDTH + 2 * KV_WIDTH + POOL_WIDTH
OUT_A_WIDTH = ATTN_WIDTH + POOL_WIDTH
CHUNK = 128
GMLP_WIDTH = D_MODEL
GMLP_GROUPS = 8
GMLP_GROUP_DIM = GMLP_WIDTH // GMLP_GROUPS
D_FF = 2816
N_MOD = 9
EPS = 1e-6
N_EVEN = (DEPTH + 1) // 2
N_ODD = DEPTH // 2


def rms_norm(x, g):
    xf = x.astype(jnp.float32)
    y = xf * lax.rsqrt(jnp.mean(xf * xf, axis=-1, keepdims=True) + EPS)
    return (y * g.astype(jnp.float32)).astype(x.dtype)

def modulate(x, g, shift, scale):
    return rms_norm(x, g) * (1 + scale) + shift

def swiglu(h, w13, w2):
    a, b = jnp.split(h @ w13, 2, axis=-1)
    return (jax.nn.silu(a) * b) @ w2

def half_ffn(x, g, shift, scale, gate, w13, w2):
    return x + 0.5 * gate * swiglu(modulate(x, g, shift, scale), w13, w2)

def axial_rope_tables(n_tokens, dtype):
    n_rows = n_tokens // GRID_W
    rows = jnp.repeat(jnp.arange(n_rows), GRID_W).astype(jnp.float32)
    cols = jnp.tile(jnp.arange(GRID_W), n_rows).astype(jnp.float32)
    half = HEAD_DIM // 2
    inv_freq = ROPE_THETA ** (-jnp.arange(0, half, 2, dtype=jnp.float32) / half)
    ang_r = rows[:, None] * inv_freq[None, :]
    ang_c = cols[:, None] * inv_freq[None, :]
    return (jnp.cos(ang_r).astype(dtype), jnp.sin(ang_r).astype(dtype),
            jnp.cos(ang_c).astype(dtype), jnp.sin(ang_c).astype(dtype))

def rope_half(x, cos, sin):
    x1, x2 = jnp.split(x, 2, axis=-1)
    cos = cos[None, :, None, :]
    sin = sin[None, :, None, :]
    return jnp.concatenate([x1 * cos - x2 * sin, x1 * sin + x2 * cos], axis=-1)

def apply_axial_rope(x, tabs):
    cr, sr, cc, sc = tabs
    xr, xc = jnp.split(x, 2, axis=-1)
    return jnp.concatenate([rope_half(xr, cr, sr), rope_half(xc, cc, sc)], axis=-1)

def gqa_attend(q, k, v):
    b, nq = q.shape[:2]
    qg = q.reshape(b, nq, N_KV_HEADS, Q_GROUP, HEAD_DIM)
    sc = jnp.einsum('bqhgd,bkhd->bhgqk', qg, k, preferred_element_type=jnp.float32) * ATTN_SCALE
    pr = jax.nn.softmax(sc, axis=-1).astype(v.dtype)
    return jnp.einsum('bhgqk,bkhd->bqhgd', pr, v).reshape(b, nq, ATTN_WIDTH)

def latent_attention(q, k_lat, v_lat, k_ctx, v_ctx):
    b, s = q.shape[:2]
    k_all = jnp.concatenate([k_ctx, k_lat], axis=1)
    v_all = jnp.concatenate([v_ctx, v_lat], axis=1)
    nb = s // Q_BLOCK
    qb = jnp.moveaxis(q.reshape(b, nb, Q_BLOCK, N_Q_HEADS, HEAD_DIM), 1, 0)
    ob = lax.map(lambda qblk: gqa_attend(qblk, k_all, v_all), qb)
    return jnp.moveaxis(ob, 0, 1).reshape(b, s, ATTN_WIDTH)

def project_a(h, w_in, qk_g):
    b, n = h.shape[:2]
    z = h @ w_in
    q = rms_norm(z[..., :ATTN_WIDTH].reshape(b, n, N_Q_HEADS, HEAD_DIM), qk_g[0])
    k = rms_norm(z[..., ATTN_WIDTH:ATTN_WIDTH + KV_WIDTH].reshape(b, n, N_KV_HEADS, HEAD_DIM), qk_g[1])
    v = z[..., ATTN_WIDTH + KV_WIDTH:ATTN_WIDTH + 2 * KV_WIDTH].reshape(b, n, N_KV_HEADS, HEAD_DIM)
    p = z[..., ATTN_WIDTH + 2 * KV_WIDTH:]
    return q, k, v, p

def project_ctx_kv(h, w_in, qk_g):
    b, n = h.shape[:2]
    z = h @ w_in[:, ATTN_WIDTH:ATTN_WIDTH + 2 * KV_WIDTH]
    k = rms_norm(z[..., :KV_WIDTH].reshape(b, n, N_KV_HEADS, HEAD_DIM), qk_g[1])
    v = z[..., KV_WIDTH:].reshape(b, n, N_KV_HEADS, HEAD_DIM)
    return k, v

def multiscale_pool(p, pool_w, pool_scale):
    n = p.shape[1]
    pf = p.astype(jnp.float32)
    cs = jnp.concatenate([jnp.zeros_like(pf[:, :1]), jnp.cumsum(pf, axis=1)], axis=1)
    t = jnp.arange(n)
    outs = []
    for gi, w in enumerate(POOL_WINDOWS):
        sl = slice(gi * POOL_GROUP_DIM, (gi + 1) * POOL_GROUP_DIM)
        lo = jnp.clip(t - w // 2, 0, n)
        hi = jnp.clip(t + w // 2, 0, n)
        csg = cs[..., sl]
        mean = (csg[:, hi] - csg[:, lo]) / (hi - lo).astype(jnp.float32)[None, :, None]
        outs.append((mean - pf[..., sl]).astype(p.dtype) @ pool_w[gi])
    return jnp.concatenate(outs, axis=-1) * pool_scale

def combine_a(attn, p, pool_w, pool_scale, w_out):
    return jnp.concatenate([attn, multiscale_pool(p, pool_w, pool_scale)], axis=-1) @ w_out

def mixer_c(h, w_in, v_g, w_sp, b_sp, w_out):
    b, n = h.shape[:2]
    z = jax.nn.gelu(h @ w_in)
    u, v = jnp.split(z, 2, axis=-1)
    v = rms_norm(v, v_g)
    vc = v.reshape(b, n // CHUNK, CHUNK, GMLP_GROUPS, GMLP_GROUP_DIM)
    sv = jnp.einsum('gpq,bnqgc->bnpgc', w_sp, vc) + b_sp.T[None, None, :, :, None]
    return (u * sv.reshape(b, n, GMLP_WIDTH)) @ w_out

def first_inputs(seed: int = 0) -> dict:
    key = jax.random.key(seed)
    ks = jax.random.split(key, 20)
    f32 = jnp.float32

    def nrm(k, shape, fan_in):
        return jax.random.normal(k, shape, f32) * (fan_in ** -0.5)

    def gain(k, shape):
        return 1.0 + 0.05 * jax.random.normal(k, shape, f32)

    return {
        "x": jax.random.normal(ks[0], (BATCH, SEQ, D_MODEL), f32),
        "c": jax.random.normal(ks[1], (BATCH, D_MODEL), f32),
        "ctx": jax.random.normal(ks[2], (BATCH, CTX_LEN, D_MODEL), f32),
        "c_ctx": jax.random.normal(ks[3], (D_MODEL,), f32),
        "w_mod": 0.5 * nrm(ks[4], (DEPTH, D_MODEL, N_MOD * D_MODEL), D_MODEL),
        "b_mod": 0.01 * jax.random.normal(ks[5], (DEPTH, N_MOD * D_MODEL), f32),
        "norm_g": gain(ks[6], (DEPTH, 3, D_MODEL)),
        "ffn_w13": nrm(ks[7], (DEPTH, 2, D_MODEL, 2 * D_FF), D_MODEL),
        "ffn_w2": nrm(ks[8], (DEPTH, 2, D_FF, D_MODEL), D_FF),
        "w_in_a": nrm(ks[9], (N_EVEN, D_MODEL, IN_A_WIDTH), D_MODEL),
        "qk_norm_g": gain(ks[10], (N_EVEN, 2, HEAD_DIM)),
        "pool_w": nrm(ks[11], (N_EVEN, len(POOL_WINDOWS), POOL_GROUP_DIM, POOL_GROUP_DIM), POOL_GROUP_DIM),
        "pool_scale": gain(ks[12], (N_EVEN, POOL_WIDTH)),
        "w_out_a": nrm(ks[13], (N_EVEN, OUT_A_WIDTH, D_MODEL), OUT_A_WIDTH),
        "w_in_c": nrm(ks[14], (N_ODD, D_MODEL, 2 * GMLP_WIDTH), D_MODEL),
        "v_norm_g": gain(ks[15], (N_ODD, GMLP_WIDTH)),
        "w_sp": nrm(ks[16], (N_ODD, GMLP_GROUPS, CHUNK, CHUNK), CHUNK),
        "b_sp": gain(ks[17], (N_ODD, GMLP_GROUPS, CHUNK)),
        "w_out_c": nrm(ks[18], (N_ODD, GMLP_WIDTH, D_MODEL), GMLP_WIDTH),
    }

def first_block(x, c, ctx, c_ctx, w_mod, b_mod, norm_g, ffn_w13, ffn_w2,
              w_in_a, qk_norm_g, pool_w, pool_scale, w_out_a,
              w_in_c, v_norm_g, w_sp, b_sp, w_out_c):
    b, s, d = x.shape
    rope_tabs = axial_rope_tables(s, x.dtype)
    silu_c = jax.nn.silu(c)
    silu_cc = jax.nn.silu(c_ctx)
    cs = ctx
    for i in range(DEPTH):
        m = (silu_c @ w_mod[i] + b_mod[i]).reshape(b, 1, N_MOD, d)
        reads_ctx = (i % 2 == 0)
        later_reads_ctx = any(j % 2 == 0 for j in range(i + 1, DEPTH))
        ctx_needed = reads_ctx or later_reads_ctx
        if ctx_needed:
            mc = (silu_cc @ w_mod[i] + b_mod[i]).reshape(1, 1, N_MOD, d)
            cs = half_ffn(cs, norm_g[i, 0], mc[:, :, 0], mc[:, :, 1], mc[:, :, 2],
                          ffn_w13[i, 0], ffn_w2[i, 0])
        x = half_ffn(x, norm_g[i, 0], m[:, :, 0], m[:, :, 1], m[:, :, 2], ffn_w13[i, 0], ffn_w2[i, 0])

        h = modulate(x, norm_g[i, 1], m[:, :, 3], m[:, :, 4])
        if i % 2 == 0:
            e = i // 2
            hc = modulate(cs, norm_g[i, 1], mc[:, :, 3], mc[:, :, 4])
            if later_reads_ctx:
                qc, kc, vc, pc = project_a(hc, w_in_a[e], qk_norm_g[e])
            else:
                kc, vc = project_ctx_kv(hc, w_in_a[e], qk_norm_g[e])
            q, k, v, p = project_a(h, w_in_a[e], qk_norm_g[e])
            q = apply_axial_rope(q, rope_tabs)
            k = apply_axial_rope(k, rope_tabs)
            attn = latent_attention(q, k, v, kc, vc)
            x = x + m[:, :, 5] * combine_a(attn, p, pool_w[e], pool_scale[e], w_out_a[e])
            if later_reads_ctx:
                attn_c = gqa_attend(qc, kc, vc)
                cs = cs + mc[:, :, 5] * combine_a(attn_c, pc, pool_w[e], pool_scale[e], w_out_a[e])
        else:
            o = i // 2
            x = x + m[:, :, 5] * mixer_c(h, w_in_c[o], v_norm_g[o], w_sp[o], b_sp[o], w_out_c[o])
            if later_reads_ctx:
                hc = modulate(cs, norm_g[i, 1], mc[:, :, 3], mc[:, :, 4])
                cs = cs + mc[:, :, 5] * mixer_c(hc, w_in_c[o], v_norm_g[o], w_sp[o], b_sp[o], w_out_c[o])

        if later_reads_ctx:
            cs = half_ffn(cs, norm_g[i, 2], mc[:, :, 6], mc[:, :, 7], mc[:, :, 8],
                          ffn_w13[i, 1], ffn_w2[i, 1])
        x = half_ffn(x, norm_g[i, 2], m[:, :, 6], m[:, :, 7], m[:, :, 8], ffn_w13[i, 1], ffn_w2[i, 1])
    return x


CHUNK_2 = 64
ROPE_BASE = 10000.0
RET_HEADS = 4
RET_DIM = 128
RET_VDIM = 128
ATT_HEADS = 8
ATT_DIM = 64
ATT_LEFT_CHUNKS = 8
REL_CLIP = 128
REL_SIZE = CHUNK_2 - 1 + REL_CLIP + 1
SB_HEADS = 16
SB_DIM = 64
SB_BLOCK = 128
N_EXPERTS = 16
N_GROUPS = 4
TOP_K = 2
D_EXPERT = 512

N_EVEN_2 = (DEPTH + 1) // 2
N_ODD_2 = DEPTH // 2
RET_W = RET_HEADS * RET_DIM
RET_VW = RET_HEADS * RET_VDIM
ATT_W = ATT_HEADS * ATT_DIM
EVEN_IN = 2 * RET_W + 2 * RET_VW + 3 * ATT_W
EVEN_MIX = RET_VW + ATT_W
EVEN_SPLITS = (RET_W, 2 * RET_W, 2 * RET_W + RET_VW, 2 * RET_W + 2 * RET_VW,
               2 * RET_W + 2 * RET_VW + ATT_W, 2 * RET_W + 2 * RET_VW + 2 * ATT_W)
SB_W = SB_HEADS * SB_DIM
ODD_IN = 3 * SB_W


def rms_norm_2(x, gain):
    xf = x.astype(jnp.float32)
    y = xf * lax.rsqrt(jnp.mean(xf * xf, axis=-1, keepdims=True) + EPS)
    return (y * gain.astype(jnp.float32)).astype(x.dtype)

def head_rms(x):
    xf = x.astype(jnp.float32)
    return xf * lax.rsqrt(jnp.mean(xf * xf, axis=-1, keepdims=True) + EPS)

def rotary(x, pos):
    d = x.shape[-1]
    inv = ROPE_BASE ** (-jnp.arange(0, d, 2, dtype=jnp.float32) / d)
    ang = pos.astype(jnp.float32)[:, None] * inv[None, :]
    cos = jnp.cos(ang)[None, :, None, :]
    sin = jnp.sin(ang)[None, :, None, :]
    x1, x2 = jnp.split(x.astype(jnp.float32), 2, axis=-1)
    return jnp.concatenate([x1 * cos - x2 * sin, x1 * sin + x2 * cos], axis=-1).astype(x.dtype)

def retention(q, k, v):
    B_, S, H, dk = q.shape
    dv = v.shape[-1]
    nc = S // CHUNK_2
    log_g = jnp.log(1.0 - 2.0 ** (-5.0 - jnp.arange(H, dtype=jnp.float32)))
    idx = jnp.arange(CHUNK_2, dtype=jnp.float32)
    intra_dec = jnp.exp(log_g[:, None, None] * jnp.abs(idx[:, None] - idx[None, :]))
    q_dec = jnp.exp(log_g[:, None] * (idx[None, :] + 1.0))
    k_dec = jnp.exp(log_g[:, None] * (CHUNK_2 - 1.0 - idx[None, :]))
    chunk_dec = jnp.exp(log_g * CHUNK_2)
    qc = q.astype(jnp.float32).reshape(B_, nc, CHUNK_2, H, dk)
    kc = k.astype(jnp.float32).reshape(B_, nc, CHUNK_2, H, dk)
    vc = v.astype(jnp.float32).reshape(B_, nc, CHUNK_2, H, dv)
    scores = jnp.einsum('bnihd,bnjhd->bnhij', qc, kc) * intra_dec
    o_intra = jnp.einsum('bnhij,bnjhe->bnihe', scores, vc)
    kv = jnp.einsum('bnjhd,hj,bnjhe->bnhde', kc, k_dec, vc)

    def step(state, kv_n):
        return state * chunk_dec[None, :, None, None] + kv_n, state

    init = jnp.zeros((B_, H, dk, dv), jnp.float32)
    _, prev = lax.scan(step, init, jnp.moveaxis(kv, 1, 0))
    prev = jnp.moveaxis(prev, 0, 1)
    o_cross = jnp.einsum('bnihd,hi,bnhde->bnihe', qc, q_dec, prev)
    return (o_intra + o_cross).reshape(B_, S, H, dv)

def chunk_attention(q, k, v, rel_bias):
    B_, S, H, d = q.shape
    nc = S // CHUNK_2
    band = ATT_LEFT_CHUNKS + 1

    def gather_band(t):
        tc = t.reshape(B_, nc, CHUNK_2, H, d)
        tp = jnp.pad(tc, ((0, 0), (ATT_LEFT_CHUNKS, 0), (0, 0), (0, 0), (0, 0)))
        return jnp.concatenate([tp[:, j:j + nc] for j in range(band)], axis=2)

    qc = q.reshape(B_, nc, CHUNK_2, H, d)
    kb = gather_band(k)
    vb = gather_band(v)
    kk = np.arange(band * CHUNK_2)
    dist = ATT_LEFT_CHUNKS * CHUNK_2 + np.arange(CHUNK_2)[:, None] - kk[None, :]
    rel_idx = np.clip(dist, -(CHUNK_2 - 1), REL_CLIP) + (CHUNK_2 - 1)
    bias = rel_bias[:, rel_idx].astype(jnp.float32)
    valid = (np.arange(nc)[:, None] - ATT_LEFT_CHUNKS + kk[None, :] // CHUNK_2) >= 0
    s = jnp.einsum('bnihd,bnkhd->bnhik', qc, kb).astype(jnp.float32) * (d ** -0.5)
    s = s + bias[None, None]
    s = jnp.where(valid[None, :, None, None, :], s, -jnp.inf)
    p = jax.nn.softmax(s, axis=-1)
    o = jnp.einsum('bnhik,bnkhd->bnihd', p, vb.astype(jnp.float32))
    return o.reshape(B_, S, H, d).astype(q.dtype)

def stick_breaking(q, k, v):
    B_, S, H, d = q.shape
    scale = d ** -0.5
    outs = []
    for blk in range(S // SB_BLOCK):
        q0 = blk * SB_BLOCK
        kend = q0 + SB_BLOCK
        z = jnp.einsum('bihd,bjhd->bhij', q[:, q0:kend], k[:, :kend]).astype(jnp.float32) * scale
        causal = jnp.arange(kend)[None, :] < (q0 + jnp.arange(SB_BLOCK))[:, None]
        log_beta = jax.nn.log_sigmoid(z)
        log_1mb = jnp.where(causal, jax.nn.log_sigmoid(-z), 0.0)
        acc = lax.cumsum(log_1mb, axis=3, reverse=True) - log_1mb
        a = jnp.where(causal, jnp.exp(log_beta + acc), 0.0)
        outs.append(jnp.einsum('bhij,bjhd->bihd', a, v[:, :kend].astype(jnp.float32)))
    return jnp.concatenate(outs, axis=1).astype(q.dtype)

def even_mixer(h, w_in, w_out, q_norm_g, k_norm_g, rel_bias, pos):
    B_, S, _ = h.shape
    proj = h @ w_in
    rq, rk, rv, rg, aq, ak, av = jnp.split(proj, EVEN_SPLITS, axis=-1)
    rq = rotary(rq.reshape(B_, S, RET_HEADS, RET_DIM), pos)
    rk = rotary(rk.reshape(B_, S, RET_HEADS, RET_DIM), pos) * (RET_DIM ** -0.5)
    ret = retention(rq, rk, rv.reshape(B_, S, RET_HEADS, RET_VDIM))
    ret = head_rms(ret).reshape(B_, S, RET_VW).astype(h.dtype) * jax.nn.silu(rg)
    aq = rms_norm_2(aq.reshape(B_, S, ATT_HEADS, ATT_DIM), q_norm_g)
    ak = rms_norm_2(ak.reshape(B_, S, ATT_HEADS, ATT_DIM), k_norm_g)
    att = chunk_attention(aq, ak, av.reshape(B_, S, ATT_HEADS, ATT_DIM), rel_bias)
    att = att.reshape(B_, S, ATT_W)
    return jnp.concatenate([ret, att], axis=-1) @ w_out

def odd_mixer(h, w_in, w_out):
    B_, S, _ = h.shape
    q, k, v = jnp.split(h @ w_in, 3, axis=-1)
    shp = (B_, S, SB_HEADS, SB_DIM)
    o = stick_breaking(q.reshape(shp), k.reshape(shp), v.reshape(shp))
    return o.reshape(B_, S, SB_W) @ w_out

def grouped_moe(h, router_w, router_b, w_gate, w_up, w_down):
    B_, S, D = h.shape
    t = h.reshape(B_ * S, D)
    scores = jax.nn.sigmoid((t @ router_w).astype(jnp.float32))
    sel = scores + router_b.astype(jnp.float32)
    per_group = N_EXPERTS // N_GROUPS
    group_score = lax.top_k(sel.reshape(-1, N_GROUPS, per_group), TOP_K)[0].sum(-1)
    best_group = jnp.argmax(group_score, axis=-1)
    in_group = (jnp.arange(N_EXPERTS) // per_group)[None, :] == best_group[:, None]
    _, top_idx = lax.top_k(jnp.where(in_group, sel, -jnp.inf), TOP_K)
    top_s = jnp.take_along_axis(scores, top_idx, axis=-1)
    top_w = top_s / jnp.sum(top_s, axis=-1, keepdims=True)
    combine = jnp.einsum('nk,nke->ne', top_w, jax.nn.one_hot(top_idx, N_EXPERTS, dtype=jnp.float32))
    y = jnp.zeros((t.shape[0], D), jnp.float32)
    for e in range(N_EXPERTS):
        he = jax.nn.silu(t @ w_gate[e]) * (t @ w_up[e])
        y = y + combine[:, e:e + 1] * (he @ w_down[e]).astype(jnp.float32)
    return y.reshape(B_, S, D).astype(h.dtype)

def second_inputs(seed: int = 0) -> dict:
    key = jax.random.key(seed)
    ks = jax.random.split(key, 20)

    def nrm(k, shape, s):
        return jax.random.normal(k, shape, jnp.float32) * s

    return {
        "x": nrm(ks[0], (BATCH, SEQ, D_MODEL), 1.0),
        "c": nrm(ks[1], (BATCH, D_MODEL), 1.0),
        "ada_w": nrm(ks[2], (DEPTH, D_MODEL, 6 * D_MODEL), 0.5 * D_MODEL ** -0.5),
        "ada_b": nrm(ks[3], (DEPTH, 6 * D_MODEL), 0.02),
        "norm1_g": 1.0 + nrm(ks[4], (DEPTH, D_MODEL), 0.02),
        "norm2_g": 1.0 + nrm(ks[5], (DEPTH, D_MODEL), 0.02),
        "even_w_in": nrm(ks[6], (N_EVEN_2, D_MODEL, EVEN_IN), D_MODEL ** -0.5),
        "even_w_out": nrm(ks[7], (N_EVEN_2, EVEN_MIX, D_MODEL), EVEN_MIX ** -0.5),
        "att_q_norm_g": 1.0 + nrm(ks[8], (N_EVEN_2, ATT_DIM), 0.02),
        "att_k_norm_g": 1.0 + nrm(ks[9], (N_EVEN_2, ATT_DIM), 0.02),
        "att_rel_bias": nrm(ks[10], (N_EVEN_2, ATT_HEADS, REL_SIZE), 0.2),
        "odd_w_in": nrm(ks[11], (N_ODD_2, D_MODEL, ODD_IN), D_MODEL ** -0.5),
        "odd_w_out": nrm(ks[12], (N_ODD_2, SB_W, D_MODEL), SB_W ** -0.5),
        "router_w": nrm(ks[13], (D_MODEL, N_EXPERTS), D_MODEL ** -0.5),
        "router_b": nrm(ks[14], (N_EXPERTS,), 0.01),
        "exp_w_gate": nrm(ks[15], (DEPTH, N_EXPERTS, D_MODEL, D_EXPERT), D_MODEL ** -0.5),
        "exp_w_up": nrm(ks[16], (DEPTH, N_EXPERTS, D_MODEL, D_EXPERT), D_MODEL ** -0.5),
        "exp_w_down": nrm(ks[17], (DEPTH, N_EXPERTS, D_EXPERT, D_MODEL), D_EXPERT ** -0.5),
    }

def second_block(x, c, ada_w, ada_b, norm1_g, norm2_g, even_w_in, even_w_out,
              att_q_norm_g, att_k_norm_g, att_rel_bias, odd_w_in, odd_w_out,
              router_w, router_b, exp_w_gate, exp_w_up, exp_w_down):
    S = x.shape[1]
    pos = jnp.arange(S, dtype=jnp.int32)
    c_act = jax.nn.silu(c)
    for layer in range(DEPTH):
        mod = (c_act @ ada_w[layer] + ada_b[layer])[:, None, :]
        sh1, sc1, g1, sh2, sc2, g2 = jnp.split(mod, 6, axis=-1)
        h = rms_norm_2(x, norm1_g[layer]) * (1.0 + sc1) + sh1
        i = layer // 2
        if layer % 2 == 0:
            mix = even_mixer(h, even_w_in[i], even_w_out[i], att_q_norm_g[i],
                             att_k_norm_g[i], att_rel_bias[i], pos)
        else:
            mix = odd_mixer(h, odd_w_in[i], odd_w_out[i])
        x = x + g1 * mix
        h = rms_norm_2(x, norm2_g[layer]) * (1.0 + sc2) + sh2
        x = x + g2 * grouped_moe(h, router_w, router_b, exp_w_gate[layer],
                                 exp_w_up[layer], exp_w_down[layer])
    return x


def setup_inputs(seed=0):
    out = dict(first_inputs(seed))
    for name, value in second_inputs(seed + 1).items():
        if name != "x":
            out[name + "_2"] = value
    return out


def reference(
    x, c, ctx, c_ctx, w_mod, b_mod, norm_g, ffn_w13, ffn_w2, w_in_a, qk_norm_g, pool_w,
    pool_scale, w_out_a, w_in_c, v_norm_g, w_sp, b_sp, w_out_c, c_2, ada_w_2, ada_b_2,
    norm1_g_2, norm2_g_2, even_w_in_2, even_w_out_2, att_q_norm_g_2, att_k_norm_g_2,
    att_rel_bias_2, odd_w_in_2, odd_w_out_2, router_w_2, router_b_2, exp_w_gate_2, exp_w_up_2,
    exp_w_down_2,
):
    x = first_block(
        x, c, ctx, c_ctx, w_mod, b_mod, norm_g, ffn_w13, ffn_w2, w_in_a, qk_norm_g, pool_w,
        pool_scale, w_out_a, w_in_c, v_norm_g, w_sp, b_sp, w_out_c,
    )
    return second_block(
        x, c_2, ada_w_2, ada_b_2, norm1_g_2, norm2_g_2, even_w_in_2, even_w_out_2,
        att_q_norm_g_2, att_k_norm_g_2, att_rel_bias_2, odd_w_in_2, odd_w_out_2, router_w_2,
        router_b_2, exp_w_gate_2, exp_w_up_2, exp_w_down_2,
    )


_drawn_inputs = setup_inputs


def setup_inputs(seed=0):
    import zlib

    import numpy as np

    out = dict(_drawn_inputs(seed))
    spreads = {}
    factors = {'qk_norm_g': 5.309,
     'norm1_g_2': 4.371,
     'att_q_norm_g_2': 5.34,
     'att_k_norm_g_2': 7.848,
     'att_rel_bias_2': 3.883}
    for name, (base, spread) in spreads.items():
        noise = np.random.default_rng([zlib.crc32(name.encode()), seed]).standard_normal(out[name].shape)
        drawn = base * np.exp(spread * noise) if base else spread * noise
        out[name] = __import__('jax').numpy.asarray(drawn.astype(out[name].dtype))
    for name, factor in factors.items():
        out[name] = (out[name] * factor).astype(out[name].dtype)
    return out
```

```python
from contextlib import ExitStack

import numpy as np

import concourse.bass as bass
from concourse import mybir

ALU = mybir.AluOpType
ACT = mybir.ActivationFunctionType
AX = mybir.AxisListType
F32 = mybir.dt.float32

P = 128
D = 1024
KT = D // P
S = 256
TT = S // P
FF = 2816
FT = FF // P
GRID_W = 64
THETA = 10000.0
EPS = 1e-6
WINDOWS = (2, 4, 8, 16)
CH = 64
NE, NG, DE = 16, 4, 512
ET = DE // P
REL = 192
BIG = 1e30

UW = KT * 2 * P
SLOTS = 4
BANK = 512

MOD_BASE = (0, 9 * KT, 18 * KT, 24 * KT)
MOD_TILES = 30 * KT

RIDERS = ((3, 20, 12), (1, 22, 72), (1, 22, 94), (1, 4, 116))

UNITS = (
    ("mod", 12), ("up0", FT + 60), ("down0", KT), ("a_in", 5), ("a_out", 4),
    ("up1", FT + 22), ("down1", KT), ("up2", FT + 22), ("down2", KT), ("c_in", 8), ("c_out", 4),
    ("up3", FT + 4), ("down3", KT), ("e_in", 14), ("e_out", 4), ("moe0", NE * 6),
    ("o_in", 12), ("o_out", 4), ("moe1", NE * 6),
)
UNIT0 = {}
_u = 0
for _name, _n in UNITS:
    UNIT0[_name] = _u
    _u += _n


def ups(f):
    riders, ridden, _ = RIDERS[f]
    u0 = UNIT0[f"up{f}"]
    parts = [(ridden, 1 + riders, u0, 0, 2 if f == 0 else 4)]
    if ridden < FT:
        parts.append((FT - ridden, 1, u0 + ridden * (1 + riders), ridden, 4))
    return parts


LIN0 = {"a_in": 0, "a_out": 5, "c_in": 9, "c_out": 17, "e_in": 21, "e_out": 35, "o_in": 39, "o_out": 51}
HEAD0 = {"a": 0, "e": 3, "r": 7}
ROT0 = {"a": 0, "e": 3}
LIN_TILE0 = {"a_in": 0, "c_in": 6, "e_in": 14, "o_in": 28}
UPDATES = {"load": 0, "down0": 16, "a_out": 24, "down1": 32, "down2": 40, "c_out": 48, "down3": 56, "e_out": 64,
           "moe0": 72, "o_out": 80, "moe1": 88}

REST = 16 * 7

_COLS = (("c", KT * 4), ("mod_b", MOD_TILES), ("norm", 10 * KT), ("pool_scale", 4), ("v_gain", KT),
         ("q_gain", 1), ("k_gain", 1), ("aq_gain", 1), ("ak_gain", 1))
COL, _c = {}, 0
for _name, _n in _COLS:
    COL[_name] = slice(_c, _c + _n)
    _c += _n
NCOLS = _c

_TABS = (("ident", P), ("flip", P), ("mean64", P), ("mean128", P), ("mean1024", P), ("rot_axial", P),
         ("rot_half", P), ("upper", P), ("ones", P), ("zeros", P), ("w4", 8), ("w16", 32),
         ("cos_axial", S), ("sin_axial", S), ("cos_half", S), ("sin_half", S),
         ("pool", 4 * TT * S), ("decay", 4 * TT * S), ("band", TT * S), ("before", 3 * P), ("after", 3 * P))
TAB, _c = {}, 0
for _name, _n in _TABS:
    TAB[_name] = slice(_c, _c + _n)
    _c += _n
NTABS = _c

NORMS = ((2 * S, 0, 0, 1, 0, "load"), (2 * S, 0, 3, 4, 1, "down0"), (S, 0, 6, 7, 2, "a_out"),
         (S, 72, 0, 1, 3, "down1"), (S, 72, 3, 4, 4, "down2"), (S, 72, 6, 7, 5, "c_out"),
         (S, 144, 0, 1, 6, "down3"), (S, 144, 3, 4, 8, "e_out"), (S, 192, 0, 1, 7, "moe0"),
         (S, 192, 3, 4, 9, "o_out"))
H_TILE0 = [0]
for _norm in NORMS:
    H_TILE0.append(H_TILE0[-1] + KT * _norm[0] // S)
FFNS = ((0, 0, 2), (2, 0, 8), (3, 72, 2), (5, 72, 8))
MOD_RUNS = ((0, 24), (24, 144), (144, 188), (188, 232), (232, 240))


def tables():
    t = {}
    i = np.arange(P)
    t["ident"] = np.eye(P)
    t["flip"] = np.eye(P)[::-1]
    t["mean64"] = (i[:, None] // 64 == i[None, :] // 64) / 64.0
    t["mean128"] = np.full((P, P), 1.0 / P)
    t["mean1024"] = np.full((P, P), 1.0 / D)
    def partner(width):
        r = np.zeros((P, P))
        for m in range(P):
            a = m % width
            if a < width // 2:
                r[m + width // 2, m] = -1.0
            else:
                r[m - width // 2, m] = 1.0
        return r
    t["rot_axial"], t["rot_half"] = partner(32), partner(P)
    t["upper"] = (i[:, None] >= i[None, :])
    t["ones"] = np.ones((P, P))
    t["zeros"] = np.zeros((P, P))
    t["w4"] = np.tile([4.0, 3.0, 2.0, 1.0], (P, 2))
    t["w16"] = np.tile(np.arange(16, 0, -1.0), (P, 2))
    n = np.arange(S)
    inv = THETA ** (-np.arange(0, 32, 2) / 32.0)
    where = np.where((i % 64)[:, None] < 32, n[None, :] // GRID_W, n[None, :] % GRID_W)
    angle = where * inv[i % 16][:, None]
    t["cos_axial"], t["sin_axial"] = np.cos(angle), np.sin(angle)
    inv = THETA ** (-np.arange(0, P, 2) / float(P))
    angle = n[None, :] * inv[i % 64][:, None]
    t["cos_half"], t["sin_half"] = np.cos(angle), np.sin(angle)
    pool = np.zeros((P, 4, TT, S))
    for g, w in enumerate(WINDOWS):
        lo, hi = np.clip(n - w // 2, 0, S), np.clip(n + w // 2, 0, S)
        m = ((n[:, None] >= lo) & (n[:, None] < hi)) / (hi - lo) - np.eye(S)
        pool[:, g] = m.reshape(TT, P, S).transpose(1, 0, 2)
    t["pool"] = pool
    gamma = 1.0 - 2.0 ** (-5.0 - np.arange(4))
    d = np.abs(n[:, None] - n[None, :])
    seen = n[:, None] // CH <= n[None, :] // CH
    decay = np.stack([np.where(seen, g ** d, 0.0) * P ** -0.5 for g in gamma])
    t["decay"] = decay.reshape(4, TT, P, S).transpose(2, 0, 1, 3)
    band = np.where(n[None, :] // CH <= n[:, None] // CH, 0.0, -BIG)
    t["band"] = band.reshape(TT, P, S).transpose(1, 0, 2)
    strict = (i[:, None] < i[None, :]).astype(float)
    before = np.concatenate([strict, np.ones((P, P)), strict], 1)
    t["before"], t["after"] = before, (before - 1.0) * BIG
    return np.concatenate([np.asarray(t[k], np.float32).reshape(P, n) for k, n in _TABS], 1)


class Line:

    def __init__(self, eng, sem):
        self.eng, self.sem, self.n = eng, sem, 0

    def __call__(self, instruction):
        instruction.then_inc(self.sem, 1)
        self.n += 1

    def wait(self):
        self.eng.wait_ge(self.sem, self.n)


def repeat(eng, n, step, body, peel=0):
    whole = n // step
    first = peel
    if whole - first < 2:
        first = whole
    for g in range(first):
        for s in range(step):
            body(g, s, g * step + s)
    if first < whole:
        with eng.Fori(first, whole) as g:
            for s in range(step):
                body(g, s, g * step + s)
    for i in range(whole * step, n):
        body(i // step, i % step, i)


def wait(eng, sem, value):
    if not isinstance(value, int) or value > 0:
        eng.wait_ge(sem, value)


def row(ap, i):
    return ap[:, bass.ds(i, 1), :].rearrange("p a n -> p (a n)")


def program(nc, x_in, cols_in, tabs_in, pool_w_in, w_sp_in, b_sp_in, router_in, router_b_in, rel_in,
            mod_w, up_w, down_w, lin_w, moe_w, ext_dram, out):
    with ExitStack() as ctx:
        def sb(name, shape):
            return ctx.enter_context(nc.sbuf_tensor(name, shape, F32))

        def sem(name):
            return ctx.enter_context(nc.semaphore(name))

        ring = sb("ring", [P, SLOTS, FT * P])
        X = sb("X", [P, KT, 2 * S])
        H = sb("H", [P, KT, 2 * S])
        G = sb("G", [P, FT, 2 * S])
        SG = sb("SG", [P, 4, BANK])
        CAT = sb("CAT", [P, KT, S])
        CB = sb("CB", [P, NE, S])
        cols = sb("cols", [P, NCOLS])
        tabs = sb("tabs", [P, NTABS])
        pool_w = sb("pool_w", [P, 4, P])
        w_sp = sb("w_sp", [P, 8, P])
        b_sp = sb("b_sp", [P, 8, P])
        router_w = sb("router_w", [P, KT, NE])
        router_b = sb("router_b", [P, TT, NE])
        rel = sb("rel", [8, REL])
        ext = sb("ext", [8, 512])
        cond = sb("cond", [P, KT, 4])
        M = sb("M", [P, MOD_TILES, 2])
        NA = sb("NA", [P, 10, 2, KT])
        HG = sb("HG", [P, 4 * 2 * KT])
        rt = sb("rt", [P, 2 * S])
        rs = sb("rs", [P, 2 * S])
        small = sb("small", [P, 64])
        eps = sb("eps", [P, 1])
        work = sb("work", [P, 24, 32])
        combT = rs[0:NE, 0:S]
        PS = ctx.enter_context(nc.psum_tensor("PS", [P, 8, BANK], F32))

        full = [sem(f"weights_full{s}") for s in range(SLOTS)]
        unit_done = sem("unit_done")
        ld_first, ld_rest, ld_ext = sem("ld_first"), sem("ld_rest"), sem("ld_ext")
        ext_ready, ext_stored = sem("ext_ready"), sem("ext_stored")
        act_line, dve_line = sem("act_line"), sem("dve_line")
        cond_ready, mods_ready = sem("cond_ready"), sem("mods_ready")
        sq_ready, ms_psum, rt_ready, xn_ready, h_ready = (
            sem(n) for n in ("sq_ready", "ms_psum", "rt_ready", "xn_ready", "h_ready"))
        silu_ready, g_ready, x_updated = sem("silu_ready"), sem("g_ready"), sem("x_updated")
        lin_ready = sem("lin_ready")
        hsq_ready, hms_psum, hrt_ready, hn_ready = (
            sem(n) for n in ("hsq_ready", "hms_psum", "hrt_ready", "hn_ready"))
        rot_psum, rot_ready = sem("rot_psum"), sem("rot_ready")
        pool_psum, pool_ready, poolw_psum = sem("pool_psum"), sem("pool_ready"), sem("poolw_psum")
        at_scores, at_max, at_exp, at_probs, at_tpsum, at_tready, at_out, at_kept = (
            sem(n) for n in ("at_scores", "at_max", "at_exp", "at_probs", "at_tpsum", "at_tready",
                             "at_out", "at_kept"))
        cat_ready = sem("cat_ready")
        v_sums, v_ready, sv_psum = sem("v_sums"), sem("v_ready"), sem("sv_psum")
        re_scores, re_decayed, re_out, re_kept = (
            sem(n) for n in ("re_scores", "re_decayed", "re_out", "re_kept"))
        sb_scores, sb_z, sb_zs, sb_log, sb_l, sb_lm, sb_sums, sb_w, sb_a, sb_out, sb_kept = (
            sem(n) for n in ("sb_scores", "sb_z", "sb_zs", "sb_log", "sb_l", "sb_lm", "sb_sums", "sb_w",
                             "sb_a", "sb_out", "sb_kept"))
        ro_psum, ro_scores, ro_comb, ro_tpsum, ro_t, ro_bpsum, ro_b = (
            sem(n) for n in ("ro_psum", "ro_scores", "ro_comb", "ro_tpsum", "ro_t", "ro_bpsum", "ro_b"))
        mo_silu, mo_weighted, mo_g, y_psum = (sem(n) for n in ("mo_silu", "mo_weighted", "mo_g", "y_psum"))
        stored, eps_ready = sem("stored"), sem("eps_ready")

        def tab(name):
            return tabs[:, TAB[name]]

        def col(name):
            return cols[:, COL[name]]

        def mod_col(base, m, d, j):
            at = base + m * KT + d
            return M[:, at, j:j + 1]

        def slot(u, k=KT):
            return ring[:, u % SLOTS, 0:UW].rearrange("p (k c) -> p k c", k=k)

        g_flat = G[:, :, :].rearrange("p a b -> p (a b)")

        def scratch(at, *shape):
            n = int(np.prod(shape))
            v = g_flat[:, at:at + n]
            if len(shape) == 1:
                return v
            if len(shape) == 2:
                return v.rearrange("p (a b) -> p a b", a=shape[0])
            return v.rearrange("p (a b c) -> p a b c", a=shape[0], b=shape[1])

        A_QK, A_SQ, A_R = scratch(0, 1536), scratch(1536, 1536), scratch(3072, 1536)
        A_V, A_P, A_POOLED = scratch(4608, 4, P), scratch(5120, TT, 512), scratch(6144, 4, S)
        PROBS, PT = scratch(7168, 4, 512), scratch(9216, 2, 512)
        C_U, C_V, C_T = scratch(0, 8, S), scratch(2048, TT, D), scratch(4096, 8, S)
        C_SQ = scratch(6144, TT, D)
        E_QK, E_G = scratch(0, 4096), scratch(4096, 1024)
        E_V = scratch(5120, TT, 1024)
        E_T, E_R = scratch(7168, 2048), scratch(9216, 2048)
        HANKEL = CB[:, 0:12, :].rearrange("p a b -> p (a b)").rearrange("p (h n) -> p h n", h=8)
        O_QK, O_V = scratch(0, 16, S), scratch(4096, TT, D)
        O_W = scratch(6144, 10, 384)

        block = ctx.enter_context(nc.Block())

        @block.sync
        def _(sp):
            def load(u, g, turns, count, width, src):
                wait(sp, unit_done, count - SLOTS)
                sp.dma_start(ring[:, u % SLOTS, 0:width], src).then_inc(full[u % SLOTS], 16)

            def source(w, i):
                return w[bass.ds(i, 1)].rearrange("a p n -> p (a n)")

            def stream(name, n, w, first, width=UW, peel=0):
                u0 = UNIT0[name]
                repeat(sp, n, SLOTS, lambda g, s, i: load(u0 + s, g, 1, i + (u0 + 1), width,
                                                          source(w, i + first)), peel)

            def up(f):
                riders, _, rider0 = RIDERS[f]
                for n, stride, u0, j0, step in ups(f):
                    def body(g, s, i):
                        load(u0 + s * stride, g, 0, i * stride + (u0 + 1), UW, source(up_w, i + (FT * f + j0)))
                        for k in range(1, stride):
                            load(u0 + s * stride + k, g, 0, i * stride + (u0 + k + 1), UW,
                                 source(mod_w, i * riders + (rider0 + k - 1)))
                    repeat(sp, n, step, body)

            def down(f):
                stream(f"down{f}", KT, down_w, KT * f, FT * P)

            stream("mod", 12, mod_w, 0, peel=1)
            up(0)
            down(0)
            stream("a_in", 5, lin_w, LIN0["a_in"])
            stream("a_out", 4, lin_w, LIN0["a_out"])
            up(1)
            down(1)
            up(2)
            down(2)
            stream("c_in", 8, lin_w, LIN0["c_in"])
            stream("c_out", 4, lin_w, LIN0["c_out"])
            up(3)
            down(3)
            stream("e_in", 14, lin_w, LIN0["e_in"])
            stream("e_out", 4, lin_w, LIN0["e_out"])
            stream("moe0", NE * 6, moe_w, 0)
            stream("o_in", 12, lin_w, LIN0["o_in"])
            stream("o_out", 4, lin_w, LIN0["o_out"])
            stream("moe1", NE * 6, moe_w, NE * 6)
            sp.wait_ge(x_updated, UPDATES["moe1"])
            sp.dma_start(out, X[:, :, 0:S]).then_inc(stored, 16)
            sp.wait_ge(stored, 16)

        @block.tensor
        def _(pe):
            mm, tr = pe.matmul, pe.transpose

            def arrived(u, g=0, turns=0):
                pe.wait_ge(full[u % SLOTS], g * (16 * turns) + 16 * (u // SLOTS + 1))

            def mod_unit(u, ct):
                w = slot(u)
                which = 2 if u >= UNIT0["up1"] else 0
                for c in range(2):
                    for k in range(KT):
                        last = mm(PS[:, 6, bass.ds(ct * 2 + 2 * c, 2)], w[:, k, c * P:(c + 1) * P],
                                  cond[:, k, which:which + 2], start=(k == 0), stop=(k == KT - 1))
                last.then_inc(unit_done, 1)

            def first_mods():
                u0 = UNIT0["mod"]
                pe.wait_ge(cond_ready, 1)

                def body(g, s, i):
                    arrived(u0 + s, g, 1)
                    mod_unit(u0 + s, i * 2)
                repeat(pe, 12, SLOTS, body)

            def norm(n):
                N = NORMS[n][0]
                for d in range(KT):
                    pe.wait_ge(sq_ready, KT * n + d + 1)
                    last = mm(PS[:, 7, 0:N], tab("mean1024"), G[:, d, 0:N], start=(d == 0), stop=(d == KT - 1))
                last.then_inc(ms_psum, 1)

            def up(f):
                N = NORMS[FFNS[f][0]][0]
                depth = 2 if N > S else 4
                pe.wait_ge(h_ready, H_TILE0[FFNS[f][0] + 1])
                pe.wait_ge(mods_ready, f + 1)
                for n, stride, u0, j0, step in ups(f):
                    turns = step * stride // SLOTS

                    def body(g, s, i):
                        u = u0 + s * stride
                        arrived(u, g, turns)
                        wait(pe, g_ready, i + (FT * f + j0 - depth + 1))
                        w = slot(u)
                        for h in range(2):
                            dst = PS[:, 2 * (s % 2) + h, :] if N > S else PS[:, s % 4, h * S:(h + 1) * S]
                            for k in range(KT):
                                last = mm(dst, w[:, k, h * P:(h + 1) * P], H[:, k, 0:N],
                                          start=(k == 0), stop=(k == KT - 1))
                        last.then_inc(unit_done, 1)
                        for r in range(1, stride):
                            arrived(u + r, g, turns)
                            mod_unit(u + r, i * (2 * RIDERS[f][0]) + 2 * (RIDERS[f][2] + r - 1))
                    repeat(pe, n, step, body, peel=(1 if f == 0 else 0))

            def down(f):
                N = NORMS[FFNS[f][0]][0]
                sides, u0 = N // S, UNIT0[f"down{f}"]
                before = UPDATES[f"down{f}"] - sides * KT
                pe.wait_ge(g_ready, FT * (f + 1))

                def body(g, s, i):
                    arrived(u0 + s, g, 1)
                    wait(pe, x_updated, i * sides + (before - 3 * sides))
                    for j in range(FT):
                        last = mm(PS[:, s, 0:N], ring[:, (u0 + s) % SLOTS, j * P:(j + 1) * P], G[:, j, 0:N],
                                  start=(j == 0), stop=(j == FT - 1))
                    last.then_inc(unit_done, 1)
                repeat(pe, KT, SLOTS, body, peel=(2 if f == 0 else 0))

            def by_features(name, n, unit, tile, src=H):
                u0, t0 = UNIT0[name] + unit, LIN_TILE0[name] + tile

                def body(g, s, i):
                    arrived(u0 + s, g, 1)
                    wait(pe, lin_ready, i + (t0 - 3))
                    w = slot(u0 + s)
                    for c in range(2):
                        for k in range(KT):
                            last = mm(PS[:, (tile + s) % 4, c * S:(c + 1) * S], w[:, k, c * P:(c + 1) * P],
                                      src[:, k, 0:S], start=(k == 0), stop=(k == KT - 1))
                    last.then_inc(unit_done, 1)
                repeat(pe, n, SLOTS, body)

            def by_tokens(name, n, unit, tile):
                u0, t0 = UNIT0[name] + unit, LIN_TILE0[name] + tile

                def body(g, s, i):
                    arrived(u0 + s, g, 1)
                    wait(pe, lin_ready, i + (t0 - 3))
                    w = slot(u0 + s)
                    for t in range(TT):
                        for k in range(KT):
                            last = mm(PS[:, (tile + s) % 4, t * S:(t + 1) * S], H[:, k, t * P:(t + 1) * P],
                                      w[:, k, :], start=(k == 0), stop=(k == KT - 1))
                    last.then_inc(unit_done, 1)
                repeat(pe, n, SLOTS, body)

            def out_proj(name):
                u0 = UNIT0[name]
                for i in range(4):
                    arrived(u0 + i)
                    w = slot(u0 + i)
                    for c in range(2):
                        for k in range(KT):
                            last = mm(PS[:, i, c * S:(c + 1) * S], w[:, k, c * P:(c + 1) * P], CAT[:, k, :],
                                      start=(k == 0), stop=(k == KT - 1))
                    last.then_inc(unit_done, 1)

            def head_norm(which, sq, n, mean):
                for c in range(n):
                    pe.wait_ge(hsq_ready, HEAD0[which] + c + 1)
                    mm(PS[:, c, :], tab(mean), sq[:, c * BANK:(c + 1) * BANK], start=True, stop=True)\
                        .then_inc(hms_psum, 1)

            def rotation(src, width, rot):
                for c in range(0, width, BANK):
                    n = min(BANK, width - c)
                    mm(PS[:, c // BANK, 0:n], tab(rot), src[:, c:c + n], start=True, stop=True)\
                        .then_inc(rot_psum, 1)

            def attention(which):
                first = 0 if which == "a" else 16
                keys = 4 if which == "a" else 2
                for s in range(18):
                    if s < 16:
                        i, half, t = s // 4, s // 2 % 2, s % 2
                        rows = slice(64 * half, 64 * half + 64)
                        if s >= 4:
                            pe.wait_ge(at_exp if which == "a" else at_max, first + s - 3)
                        if which == "a":
                            mm(PS[:, s % 4, :], A_QK[rows, i * S + t * P:i * S + t * P + P],
                               A_QK[rows, 4 * S:6 * S], start=True, stop=True).then_inc(at_scores, 1)
                        else:
                            q0 = 2048 + i * S + t * P
                            mm(PS[:, s % 4, 0:S], E_QK[rows, q0:q0 + P],
                               E_QK[rows, 3072 + i * S:3072 + (i + 1) * S], start=True, stop=False)
                            mm(PS[:, s % 4, 0:S], tab("flip"), HANKEL[:, 2 * i + half, P - P * t:P - P * t + S],
                               start=False, stop=True).then_inc(at_scores, 1)
                    if 1 <= s <= 16:
                        it = s - 1
                        pe.wait_ge(at_probs, first + it + 1)
                        if it >= 2:
                            pe.wait_ge(at_tready, first + it - 1)
                        for k in range(keys):
                            last = tr(PS[:, 4 + it % 2, k * P:(k + 1) * P], PROBS[:, it % 4, k * P:(k + 1) * P],
                                      tab("ident"))
                        last.then_inc(at_tpsum, 1)
                    if s >= 2:
                        it = s - 2
                        i, half, t = it // 4, it // 2 % 2, it % 2
                        pe.wait_ge(at_tready, first + it + 1)
                        if it % 4 == 0 and i >= 2:
                            pe.wait_ge(at_kept, first // 4 + i - 1)
                        for k in range(keys):
                            if which == "a":
                                v = A_V[:, k, 64 * half:64 * half + 64]
                            else:
                                v = E_V[:, k, 512 + (2 * i + half) * 64:512 + (2 * i + half) * 64 + 64]
                            last = mm(PS[64 * half:64 * half + 64, 6 + i % 2, t * P:(t + 1) * P], v,
                                      PT[:, it % 2, k * P:(k + 1) * P], start=(k == 0), stop=(k == keys - 1))
                        last.then_inc(at_out, 1)

            def mixer_a():
                u0 = UNIT0["a_in"]
                pe.wait_ge(h_ready, H_TILE0[2])
                by_features("a_in", 2, 0, 0)
                arrived(u0 + 2)
                w = slot(u0 + 2)
                for k in range(KT):
                    mm(PS[:, 2, :], w[:, k, 0:P], H[:, k, :], start=(k == 0), stop=(k == KT - 1))
                for t in range(2 * TT):
                    for k in range(KT):
                        last = mm(PS[:, 3, t * P:(t + 1) * P], H[:, k, t * P:(t + 1) * P], w[:, k, P:2 * P],
                                  start=(k == 0), stop=(k == KT - 1))
                last.then_inc(unit_done, 1)
                by_tokens("a_in", 2, 3, 4)
                head_norm("a", A_SQ, 3, "mean64")
                pe.wait_ge(mods_ready, 2)
                for g in range(4):
                    for t in range(TT):
                        last = mm(PS[:, 4 + g // 2, (g % 2) * S:(g % 2 + 1) * S], A_P[:, t, g * P:(g + 1) * P],
                                  tab("pool").rearrange("p (g t n) -> p g t n", g=4, t=TT)[:, g, t, :],
                                  start=(t == 0), stop=(t == TT - 1))
                last.then_inc(pool_psum, 1)
                pe.wait_ge(pool_ready, 2)
                for g in range(4):
                    last = mm(PS[:, 6 + g // 2, (g % 2) * S:(g % 2 + 1) * S], pool_w[:, g, :], A_POOLED[:, g, :],
                              start=True, stop=True)
                last.then_inc(poolw_psum, 1)
                pe.wait_ge(hn_ready, 3)
                rotation(A_QK, 5 * S, "rot_axial")
                pe.wait_ge(rot_ready, 3)
                pe.wait_ge(cat_ready, 1)
                attention("a")
                pe.wait_ge(at_kept, 4)
                out_proj("a_out")

            def mixer_c():
                pe.wait_ge(h_ready, H_TILE0[5])
                by_features("c_in", 4, 0, 0)
                by_tokens("c_in", 4, 4, 4)
                pe.wait_ge(v_ready, 2)
                for g in range(8):
                    for t in range(TT):
                        last = mm(PS[:, 4 + g // 2, (g % 2) * S + t * P:(g % 2) * S + (t + 1) * P],
                                  C_V[:, t, g * P:(g + 1) * P], w_sp[:, g, :], start=True, stop=True)
                    if g % 2:
                        last.then_inc(sv_psum, 1)
                pe.wait_ge(cat_ready, 2)
                out_proj("c_out")

            def mixer_e():
                pe.wait_ge(h_ready, H_TILE0[7])
                by_features("e_in", 10, 0, 0)
                by_tokens("e_in", 4, 10, 10)
                pe.wait_ge(lin_ready, LIN_TILE0["e_in"] + 14)
                rotation(E_QK, 2048, "rot_half")
                pe.wait_ge(rot_ready, 7)
                head_norm("e", E_T, 4, "mean64")
                pe.wait_ge(hrt_ready, HEAD0["e"] + 4)
                for h in range(4):
                    for t in range(TT):
                        last = mm(PS[:, h, t * S:(t + 1) * S], E_QK[:, 1024 + h * S + t * P:1024 + h * S + (t + 1) * P],
                                  E_QK[:, h * S:(h + 1) * S], start=True, stop=True)
                    last.then_inc(re_scores, 1)
                for h in range(4):
                    pe.wait_ge(re_decayed, h + 1)
                    for t in range(TT):
                        last = mm(PS[:, 4 + h // 2, (h % 2) * S:(h % 2 + 1) * S], E_V[:, t, h * P:(h + 1) * P],
                                  SG[:, h, t * S:(t + 1) * S], start=(t == 0), stop=(t == TT - 1))
                    last.then_inc(re_out, 1)
                head_norm("r", E_T[:, 1024:2048], 2, "mean128")
                pe.wait_ge(cat_ready, 4)
                pe.wait_ge(ld_ext, 16)
                attention("e")
                pe.wait_ge(at_kept, 8)
                out_proj("e_out")

            def mixer_o():
                pe.wait_ge(h_ready, H_TILE0[9])
                by_features("o_in", 8, 0, 0)
                by_tokens("o_in", 4, 8, 8)
                pe.wait_ge(lin_ready, LIN_TILE0["o_in"] + 12)
                for s in range(18):
                    if s < 16:
                        h, rows, tile = s, slice(64 * (s % 2), 64 * (s % 2) + 64), s // 2
                        q, k = O_QK[rows, tile, :], O_QK[rows, 8 + tile, :]
                        if h >= 2:
                            pe.wait_ge(sb_z, h - 1)
                        mm(PS[:, h % 2, 0:S], k[:, 0:P], q, start=True, stop=True)
                        mm(PS[:, h % 2, S:S + P], k[:, P:S], q[:, P:S], start=True, stop=True)\
                            .then_inc(sb_scores, 1)
                    if 1 <= s <= 16:
                        h = s - 1
                        lm = O_W[:, 5 * (h % 2) + 3, :]
                        pe.wait_ge(sb_lm, h + 1)
                        if h >= 2:
                            pe.wait_ge(sb_w, h - 1)
                        mm(PS[:, 2 + h % 2, 0:S], tab("upper"), lm[:, 0:S], start=True, stop=False)
                        mm(PS[:, 2 + h % 2, P:S], tab("ones"), lm[:, S:S + P], start=False, stop=True)
                        mm(PS[:, 2 + h % 2, S:S + P], tab("upper"), lm[:, S:S + P], start=True, stop=True)\
                            .then_inc(sb_sums, 1)
                    if s >= 2:
                        h, rows, tile = s - 2, slice(64 * (s % 2), 64 * (s % 2) + 64), (s - 2) // 2
                        a = O_W[:, 5 * (h % 2) + 4, :]
                        pe.wait_ge(sb_a, h + 1)
                        if h % 2 == 0 and tile >= 2:
                            pe.wait_ge(sb_kept, tile - 1)
                        mm(PS[rows, 4 + tile % 2, 0:S], O_V[:, 0, 64 * h:64 * h + 64], a[:, 0:S],
                           start=True, stop=False)
                        mm(PS[rows, 4 + tile % 2, P:S], O_V[:, 1, 64 * h:64 * h + 64], a[:, S:S + P],
                           start=False, stop=True).then_inc(sb_out, 1)
                pe.wait_ge(sb_kept, 8)
                out_proj("o_out")

            def moe(l):
                u0 = UNIT0[f"moe{l}"]
                pe.wait_ge(h_ready, H_TILE0[8 + 2 * l])
                for t in range(TT):
                    for k in range(KT):
                        last = mm(PS[:, 0, t * NE:(t + 1) * NE], H[:, k, t * P:(t + 1) * P], router_w[:, k, :],
                                  start=(k == 0), stop=(k == KT - 1))
                last.then_inc(ro_psum, 1)
                pe.wait_ge(ro_comb, l + 1)
                comb = work[:, 22, :].rearrange("p (t e) -> p t e", t=TT)
                for t in range(TT):
                    last = tr(PS[0:NE, 1, t * P:(t + 1) * P], comb[:, t, :], tab("ident"))
                last.then_inc(ro_tpsum, 1)
                pe.wait_ge(ro_t, l + 1)
                for e in range(NE):
                    if e % 2 == 0 and e >= 8:
                        pe.wait_ge(ro_b, 8 * l + e // 2 - 3)
                    last = mm(PS[:, e // 2 % 4, (e % 2) * S:(e % 2 + 1) * S],
                              tabs[0:NE, TAB["ident"]][:, e:e + 1].to_broadcast([NE, P]), combT,
                              start=True, stop=True)
                    if e % 2:
                        last.then_inc(ro_bpsum, 1)
                pe.wait_ge(ro_b, 8 * (l + 1))
                for b in range(4):
                    mm(PS[:, 4 + b, :], tab("zeros"), tabs[:, 0:BANK], start=True, stop=False, skip_group_check=True)

                def body(g, s, e):
                    for f in range(ET):
                        arrived(u0 + 6 * s + f, g, 3)
                        wait(pe, mo_g, e * 4 + (4 * NE * l + f - 3))
                        w = slot(u0 + 6 * s + f)
                        for h in range(2):
                            for k in range(KT):
                                last = mm(PS[:, f, h * S:(h + 1) * S], w[:, k, h * P:(h + 1) * P], H[:, k, 0:S],
                                          start=(k == 0), stop=(k == KT - 1))
                        last.then_inc(unit_done, 1)
                    for h in range(2):
                        u = u0 + 6 * s + 4 + h
                        arrived(u, g, 3)
                        pe.wait_ge(mo_g, e * 4 + (4 * NE * l + 2 * h + 2))
                        for f in range(2):
                            for d in range(KT):
                                last = mm(PS[:, 4 + d // 2, (d % 2) * S:(d % 2 + 1) * S],
                                          ring[:, u % SLOTS, f * D + d * P:f * D + (d + 1) * P],
                                          G[:, 4 * s + 2 * h + f, 0:S], start=False, stop=False,
                                          skip_group_check=True)
                        last.then_inc(unit_done, 1)
                repeat(pe, NE, 2, body, peel=(1 if l == 0 else 0))
                for b in range(4):
                    last = mm(PS[:, 4 + b, :], tab("zeros"), tabs[:, 0:BANK], start=False, stop=True,
                              skip_group_check=True)
                last.then_inc(y_psum, 1)

            first_mods()
            pe.wait_ge(ld_rest, REST)
            norm(0)
            up(0)
            down(0)
            norm(1)
            mixer_a()
            norm(2)
            up(1)
            down(1)
            norm(3)
            up(2)
            down(2)
            norm(4)
            mixer_c()
            norm(5)
            up(3)
            down(3)
            norm(6)
            mixer_e()
            norm(7)
            moe(0)
            norm(8)
            mixer_o()
            norm(9)
            moe(1)

        @block.scalar
        def _(act):
            line = Line(act, act_line)
            af = act.activation

            def norm(n):
                N, base, shift, _, _, before = NORMS[n]
                wait(act, x_updated, UPDATES[before])
                for d in range(KT):
                    af(G[:, d, 0:N], X[:, d, 0:N], ACT.Square).then_inc(sq_ready, 1)
                act.wait_ge(ms_psum, n + 1)
                af(rt[:, 0:N], PS[:, 7, 0:N], ACT.Sqrt, bias=eps[:, 0:1]).then_inc(rt_ready, 1)
                for d in range(KT):
                    act.wait_ge(xn_ready, KT * n + d + 1)
                    for j in range(N // S):
                        h = H[:, d, j * S:(j + 1) * S]
                        af(h, h, ACT.Identity, scale=NA[:, n, j, d:d + 1],
                           bias=mod_col(base, shift, d, j)).then_inc(h_ready, 1)

            def up(f):
                N = NORMS[FFNS[f][0]][0]
                for n, stride, u0, j0, step in ups(f):
                    def body(g, s, i):
                        act.wait_ge(unit_done, i * stride + (u0 + 1))
                        wait(act, g_ready, i + (FT * f + j0 - step + 1))
                        src = PS[:, 2 * (s % 2), :] if N > S else PS[:, s % 4, 0:S]
                        af(SG[:, s % 4, 0:N], src, ACT.Silu).then_inc(silu_ready, 1)
                    repeat(act, n, step, body, peel=(1 if f == 0 else 0))

            def evacuate(name, tile, unit, dst, src_width=BANK, func=ACT.Copy):
                act.wait_ge(unit_done, UNIT0[name] + unit + 1)
                src = PS[:, tile % 4, :]
                if len(dst.shape) == 3:
                    src = src.rearrange("p (t n) -> p t n", t=dst.shape[1])
                af(dst, src, func).then_inc(lin_ready, 1)

            def head_norm(which, src, sq, r, n):
                for c in range(n):
                    w = slice(c * BANK, (c + 1) * BANK)
                    af(sq[:, w], src[:, w], ACT.Square).then_inc(hsq_ready, 1)
                for c in range(n):
                    act.wait_ge(hms_psum, HEAD0[which] + c + 1)
                    af(r[:, c * BANK:(c + 1) * BANK], PS[:, c, :], ACT.Sqrt, bias=eps[:, 0:1])\
                        .then_inc(hrt_ready, 1)

            def attention(which):
                first = 0 if which == "a" else 16
                keys, cat0 = (4, 0) if which == "a" else (2, 4)
                W = keys * P
                for s in range(18):
                    if s < 16:
                        act.wait_ge(at_max, first + s + 1)
                        if s >= 4:
                            act.wait_ge(at_tpsum, first + s - 3)
                        src = PS[:, s % 4, :] if which == "a" else PROBS[:, s % 4, 0:W]
                        af(PROBS[:, s % 4, 0:W], src, ACT.Exp, scale=(0.125 if which == "a" else 1.0),
                           bias=small[:, 4 + s % 4:5 + s % 4], accum_out=small[:, 8 + s % 4:9 + s % 4])\
                            .then_inc(at_exp, 1)
                    if 1 <= s <= 16:
                        it = s - 1
                        act.wait_ge(at_tpsum, first + it + 1)
                        if it >= 2:
                            act.wait_ge(at_out, first + it - 1)
                        af(PT[:, it % 2, 0:W], PS[:, 4 + it % 2, 0:W], ACT.Copy).then_inc(at_tready, 1)
                    if s >= 2 and (s - 2) % 4 == 3:
                        i = (s - 2) // 4
                        act.wait_ge(at_out, first + 4 * i + 4)
                        af(CAT[:, cat0 + i, :], PS[:, 6 + i % 2, 0:S], ACT.Copy).then_inc(at_kept, 1)

            def mixer_a():
                for t, u in enumerate((0, 1, 2)):
                    evacuate("a_in", t, u, A_QK[:, t * BANK:(t + 1) * BANK])
                evacuate("a_in", 3, 2, A_V[:, :, :])
                for t, u in ((4, 3), (5, 4)):
                    evacuate("a_in", t, u, A_P[:, :, (t - 4) * S:(t - 3) * S])
                act.wait_ge(lin_ready, 6)
                head_norm("a", A_QK, A_SQ, A_R, 3)
                act.wait_ge(pool_psum, 1)
                for c in range(2):
                    af(A_POOLED[:, 2 * c:2 * c + 2, :], PS[:, 4 + c, :].rearrange("p (g n) -> p g n", g=2),
                       ACT.Copy).then_inc(pool_ready, 1)
                act.wait_ge(cat_ready, 1)
                attention("a")

            def mixer_c():
                for t in range(4):
                    evacuate("c_in", t, t, C_U[:, 2 * t:2 * t + 2, :], func=ACT.Gelu_apprx_tanh)
                for t in range(4):
                    evacuate("c_in", 4 + t, 4 + t, C_V[:, :, t * S:(t + 1) * S], func=ACT.Gelu_apprx_tanh)
                act.wait_ge(lin_ready, LIN_TILE0["c_in"] + 8)
                for t in range(TT):
                    line(af(C_SQ[:, t, :], C_V[:, t, :], ACT.Square, accum_out=small[:, 16 + t:17 + t]))
                line.wait()
                af(small[:, 18:20], small[:, 16:18], ACT.Sqrt, scale=1.0 / D, bias=eps[:, 0:1]).then_inc(v_sums, 1)

            def mixer_e():
                for t in range(8):
                    evacuate("e_in", t, t, E_QK[:, t * BANK:(t + 1) * BANK])
                for t in (8, 9):
                    evacuate("e_in", t, t, E_G[:, (t - 8) * BANK:(t - 7) * BANK], func=ACT.Silu)
                for t in range(10, 14):
                    evacuate("e_in", t, t, E_V[:, :, (t - 10) * S:(t - 9) * S])
                act.wait_ge(lin_ready, LIN_TILE0["e_in"] + 14)
                act.wait_ge(rot_ready, 7)
                head_norm("e", E_QK[:, 2048:4096], E_T, E_R, 4)
                act.wait_ge(hn_ready, HEAD0["e"] + 4)
                for c in range(2):
                    act.wait_ge(re_out, 2 * c + 2)
                    af(E_T[:, c * BANK:(c + 1) * BANK], PS[:, 4 + c, :], ACT.Copy).then_inc(re_kept, 1)
                act.wait_ge(re_kept, 2)
                head_norm("r", E_T[:, 0:1024], E_T[:, 1024:2048], E_R, 2)
                act.wait_ge(cat_ready, 4)
                attention("e")

            def mixer_o():
                for t in range(8):
                    evacuate("o_in", t, t, O_QK[:, 2 * t:2 * t + 2, :])
                for t in range(8, 12):
                    evacuate("o_in", t, t, O_V[:, :, (t - 8) * S:(t - 7) * S])
                for s in range(18):
                    if s < 16:
                        e = O_W[:, 5 * (s % 2) + 2, :]
                        act.wait_ge(sb_z, s + 1)
                        if s >= 2:
                            act.wait_ge(sb_l, s - 1)
                        line(af(e, O_W[:, 5 * (s % 2), :], ACT.Abs))
                        line.wait()
                        line(af(e, e, ACT.Exp, scale=-1.0))
                        line.wait()
                        af(e, e, ACT.Ln, bias=1.0).then_inc(sb_log, 1)
                    if 1 <= s <= 16:
                        h = s - 1
                        a = O_W[:, 5 * (h % 2) + 4, :]
                        act.wait_ge(sb_w, h + 1)
                        af(a, a, ACT.Exp).then_inc(sb_a, 1)
                    if s >= 2 and s % 2:
                        tile = (s - 2) // 2
                        act.wait_ge(sb_out, 2 * tile + 2)
                        af(CAT[:, tile, :], PS[:, 4 + tile % 2, 0:S], ACT.Copy).then_inc(sb_kept, 1)

            def moe(l):
                u0 = UNIT0[f"moe{l}"]
                act.wait_ge(ro_psum, l + 1)
                af(work[:, 0, :], PS[:, 0, 0:TT * NE], ACT.Sigmoid).then_inc(ro_scores, 1)
                act.wait_ge(ro_tpsum, l + 1)
                af(combT, PS[0:NE, 1, 0:S], ACT.Copy).then_inc(ro_t, 1)
                for c in range(8):
                    act.wait_ge(ro_bpsum, 8 * l + c + 1)
                    af(CB[:, 2 * c:2 * c + 2, :], PS[:, c % 4, :].rearrange("p (e n) -> p e n", e=2), ACT.Copy)\
                        .then_inc(ro_b, 1)

                def body(g, s, e):
                    for f in range(ET):
                        act.wait_ge(unit_done, e * 6 + (u0 + f + 1))
                        wait(act, mo_weighted, e * 4 + (4 * NE * l + f - 3))
                        af(SG[:, f, 0:S], PS[:, f, 0:S], ACT.Silu).then_inc(mo_silu, 1)
                repeat(act, NE, 2, body, peel=(1 if l == 0 else 0))

            act.dma_start(cols[:, :], cols_in).then_inc(ld_first, 16)
            act.dma_start(X[:, :, :], x_in).then_inc(ld_first, 16)
            for dst, src in ((tabs[:, :], tabs_in), (rel[:, :], rel_in), (router_w[:, :, :], router_in),
                             (router_b[:, :, :], router_b_in), (pool_w[:, :, :], pool_w_in),
                             (w_sp[:, :, :], w_sp_in), (b_sp[:, :, :], b_sp_in)):
                act.dma_start(dst, src).then_inc(ld_rest, 16)
            act.wait_ge(ld_first, 32)
            af(cond[:, :, :].rearrange("p k c -> p (k c)"), col("c"), ACT.Silu).then_inc(cond_ready, 1)
            act.wait_ge(eps_ready, 1)
            norm(0)
            up(0)
            norm(1)
            mixer_a()
            norm(2)
            up(1)
            norm(3)
            up(2)
            norm(4)
            mixer_c()
            norm(5)
            up(3)
            norm(6)
            mixer_e()
            norm(7)
            moe(0)
            norm(8)
            mixer_o()
            norm(9)
            moe(1)

        @block.gpsimd
        def _(pool):
            pool.memset(eps[:, :], EPS).then_inc(eps_ready, 1)
            pool.wait_ge(ext_ready, 3)
            pool.dma_start(ext_dram, ext[:, :]).then_inc(ext_stored, 16)
            pool.wait_ge(ext_stored, 16)
            pool.dma_start(HANKEL, bass.AP(ext_dram.tensor, 0, [[1, P], [512, 8], [1, 384]])).then_inc(ld_ext, 16)

            pool.wait_ge(ld_rest, REST)
            for h in range(16):
                z, zs, lm = (O_W[:, 5 * (h % 2) + i, :] for i in (0, 1, 3))
                pool.wait_ge(sb_z, h + 1)
                if h >= 2:
                    pool.wait_ge(sb_w, h - 1)
                pool.tensor_tensor(zs, z, tab("after"), ALU.add).then_inc(sb_zs, 1)
                pool.wait_ge(sb_l, h + 1)
                pool.tensor_tensor(lm, lm, tab("before"), ALU.mult).then_inc(sb_lm, 1)

        @block.vector
        def _(dve):
            line = Line(dve, dve_line)
            tt, ts, stt = dve.tensor_tensor, dve.tensor_scalar, dve.scalar_tensor_tensor

            def take_mods(run, u):
                a, b = MOD_RUNS[run]
                dve.wait_ge(unit_done, u + 1)
                bias = cols[:, COL["mod_b"].start + a:COL["mod_b"].start + b]
                src = PS[:, 6, 2 * a:2 * b].rearrange("p (n j) -> p n j", j=2)
                line(tt(M[:, a:b, 0], src[:, :, 0], bias, ALU.add))
                tt(M[:, a:b, 1], src[:, :, 1], bias, ALU.add).then_inc(mods_ready, 1)
                dve.wait_ge(mods_ready, run + 1)
                line.wait()

            def norm_columns(n):
                N, base, _, scale, gain, _ = NORMS[n]
                g = cols[:, COL["norm"].start + gain * KT:COL["norm"].start + (gain + 1) * KT]
                for j in range(N // S):
                    at = base + scale * KT
                    line(stt(out=NA[:, n, j, :], in0=M[:, at:at + KT, j], scalar=1.0, in1=g,
                             op0=ALU.add, op1=ALU.mult))

            def norm(n):
                N = NORMS[n][0]
                norm_columns(n)
                dve.wait_ge(rt_ready, n + 1)
                line(dve.reciprocal(rs[:, 0:N], rt[:, 0:N]))
                line.wait()
                for d in range(KT):
                    tt(H[:, d, 0:N], X[:, d, 0:N], rs[:, 0:N], ALU.mult).then_inc(xn_ready, 1)

            def up(f):
                N = NORMS[FFNS[f][0]][0]
                for n, stride, u0, j0, step in ups(f):
                    def body(g, s, i):
                        dve.wait_ge(silu_ready, i + (FT * f + j0 + 1))
                        src = PS[:, 2 * (s % 2) + 1, :] if N > S else PS[:, s % 4, S:2 * S]
                        tt(row(G[:, :, 0:N], i + j0), SG[:, s % 4, 0:N], src, ALU.mult).then_inc(g_ready, 1)
                    repeat(dve, n, step, body)

            def down(f):
                N = NORMS[FFNS[f][0]][0]
                _, base, gate = FFNS[f]
                u0 = UNIT0[f"down{f}"]
                at = base + gate * KT
                for j in range(N // S):
                    line(ts(HG[:, (2 * f + j) * KT:(2 * f + j + 1) * KT], M[:, at:at + KT, j], 0.5, None, ALU.mult))
                line.wait()

                def body(g, s, i):
                    dve.wait_ge(unit_done, i + (u0 + 1))
                    for j in range(N // S):
                        x = X[:, bass.ds(i, 1), j * S:(j + 1) * S].rearrange("p a n -> p (a n)")
                        stt(out=x, in0=PS[:, s, j * S:(j + 1) * S], scalar=HG[:, bass.ds(i + (2 * f + j) * KT, 1)],
                            in1=x, op0=ALU.mult, op1=ALU.add).then_inc(x_updated, 1)
                repeat(dve, KT, SLOTS, body)

            def add_out(name, base, gate):
                for d in range(KT):
                    if d % 2 == 0:
                        dve.wait_ge(unit_done, UNIT0[name] + d // 2 + 1)
                    stt(out=X[:, d, 0:S], in0=PS[:, d // 2, (d % 2) * S:(d % 2 + 1) * S],
                        scalar=mod_col(base, gate, d, 0), in1=X[:, d, 0:S], op0=ALU.mult, op1=ALU.add)\
                        .then_inc(x_updated, 1)

            def head_norm(which, src, r, gains):
                for c, gain in enumerate(gains):
                    w = slice(c * BANK, (c + 1) * BANK)
                    dve.wait_ge(hrt_ready, HEAD0[which] + c + 1)
                    line(dve.reciprocal(r[:, w], r[:, w]))
                    line.wait()
                    if gain is None:
                        tt(src[:, w], src[:, w], r[:, w], ALU.mult).then_inc(hn_ready, 1)
                    else:
                        stt(out=src[:, w], in0=src[:, w], scalar=gain, in1=r[:, w], op0=ALU.mult, op1=ALU.mult)\
                            .then_inc(hn_ready, 1)

            def rotation(which, src, width, t, r, cos, sin):
                for c in range(0, width, BANK):
                    n = min(BANK, width - c)
                    tiles = lambda ap: ap[:, c:c + n].rearrange("p (a n) -> p a n", n=S)
                    wide = lambda name: tab(name).unsqueeze(1).to_broadcast([P, n // S, S])
                    line(tt(tiles(t), tiles(src), wide(cos), ALU.mult))
                    dve.wait_ge(rot_psum, ROT0[which] + c // BANK + 1)
                    line(tt(tiles(r), PS[:, c // BANK, 0:n].rearrange("p (a n) -> p a n", n=S), wide(sin), ALU.mult))
                    line.wait()
                    tt(src[:, c:c + n], t[:, c:c + n], r[:, c:c + n], ALU.add).then_inc(rot_ready, 1)

            def attention(which):
                first = 0 if which == "a" else 16
                W = 4 * P if which == "a" else 2 * P
                for s in range(17):
                    if s < 16:
                        top, neg = small[:, s % 4:s % 4 + 1], small[:, 4 + s % 4:5 + s % 4]
                        dve.wait_ge(at_scores, first + s + 1)
                        scores = PS[:, s % 4, 0:W]
                        if which == "e":
                            if s >= 4:
                                dve.wait_ge(at_tpsum, first + s - 3)
                            line(tt(PROBS[:, s % 4, 0:W], scores,
                                    tab("band").rearrange("p (t n) -> p t n", t=TT)[:, s % 2, :], ALU.add))
                            line.wait()
                            scores = PROBS[:, s % 4, 0:W]
                        line(dve.tensor_reduce(top, scores, AX.X, ALU.max))
                        line.wait()
                        ts(neg, top, -0.125 if which == "a" else -1.0, None, ALU.mult).then_inc(at_max, 1)
                    if s >= 1:
                        it = s - 1
                        dve.wait_ge(at_exp, first + it + 1)
                        line(dve.reciprocal(small[:, 12 + it % 4:13 + it % 4], small[:, 8 + it % 4:9 + it % 4]))
                        line.wait()
                        ts(PROBS[:, it % 4, 0:W], PROBS[:, it % 4, 0:W], small[:, 12 + it % 4:13 + it % 4], None,
                           ALU.mult).then_inc(at_probs, 1)

            def mixer_a():
                head_norm("a", A_QK, A_R, (col("q_gain"), col("q_gain"), col("k_gain")))
                dve.wait_ge(hn_ready, 3)
                dve.wait_ge(poolw_psum, 1)
                for g in range(4):
                    last = ts(CAT[:, 4 + g, :], PS[:, 6 + g // 2, (g % 2) * S:(g % 2 + 1) * S],
                              cols[:, COL["pool_scale"].start + g:COL["pool_scale"].start + g + 1], None, ALU.mult)
                last.then_inc(cat_ready, 1)
                rotation("a", A_QK, 5 * S, A_SQ, A_R, "cos_axial", "sin_axial")
                attention("a")
                add_out("a_out", 0, 5)

            def mixer_c():
                dve.wait_ge(v_sums, 1)
                line(dve.reciprocal(small[:, 20:22], small[:, 18:20]))
                line.wait()
                for t in range(TT):
                    ts(C_V[:, t, :], C_V[:, t, :], small[:, 20 + t:21 + t], None, ALU.mult).then_inc(v_ready, 1)
                for g in range(8):
                    if g % 2 == 0:
                        dve.wait_ge(sv_psum, g // 2 + 1)
                    src = PS[:, 4 + g // 2, (g % 2) * S:(g % 2 + 1) * S].rearrange("p (t n) -> p t n", t=TT)
                    line(stt(out=C_T[:, g, :].rearrange("p (t n) -> p t n", t=TT), in0=src,
                             scalar=cols[:, COL["v_gain"].start + g:COL["v_gain"].start + g + 1],
                             in1=b_sp[:, g, :].unsqueeze(1).to_broadcast([P, TT, P]), op0=ALU.mult, op1=ALU.add))
                line.wait()
                dve.tensor_tensor(CAT[:, :, :], C_T[:, :, :], C_U[:, :, :], ALU.mult).then_inc(cat_ready, 1)
                add_out("c_out", 72, 5)

            def mixer_e():
                line(ts(small[:, 24:25], col("aq_gain"), 0.125, None, ALU.mult))
                dve.wait_ge(lin_ready, LIN_TILE0["e_in"] + 4)
                rotation("e", E_QK, 2048, E_T, E_R, "cos_half", "sin_half")
                head_norm("e", E_QK[:, 2048:4096], E_R, (small[:, 24:25],) * 2 + (col("ak_gain"),) * 2)
                for h in range(4):
                    dve.wait_ge(re_scores, h + 1)
                    tt(SG[:, h, :], PS[:, h, :], tab("decay")[:, h * BANK:(h + 1) * BANK], ALU.mult)\
                        .then_inc(re_decayed, 1)
                head_norm("r", E_T[:, 0:1024], E_R, (None, None))
                dve.wait_ge(hn_ready, HEAD0["r"] + 2)
                for c in range(2):
                    w = slice(c * BANK, (c + 1) * BANK)
                    tt(CAT[:, 2 * c:2 * c + 2, :].rearrange("p a n -> p (a n)"), E_T[:, w], E_G[:, w], ALU.mult)\
                        .then_inc(cat_ready, 1)
                dve.wait_ge(cat_ready, 4)
                attention("e")
                add_out("e_out", 144, 2)

            def mixer_o():
                for s in range(17):
                    if s < 16:
                        z = O_W[:, 5 * (s % 2), :]
                        dve.wait_ge(sb_scores, s + 1)
                        if s >= 2:
                            dve.wait_ge(sb_zs, s - 1)
                        ts(z, PS[:, s % 2, 0:384], 0.125, None, ALU.mult).then_inc(sb_z, 1)
                    if s >= 1:
                        h = s - 1
                        dve.wait_ge(sb_sums, h + 1)
                        if h >= 2:
                            dve.wait_ge(sb_out, h - 1)
                        tt(O_W[:, 5 * (h % 2) + 4, :], O_W[:, 5 * (h % 2) + 1, :], PS[:, 2 + h % 2, 0:384],
                           ALU.subtract).then_inc(sb_w, 1)
                    if s < 16:
                        dve.wait_ge(sb_log, s + 1)
                        dve.wait_ge(sb_z, s + 1)
                        stt(out=O_W[:, 5 * (s % 2) + 3, :], in0=z, scalar=0.0, in1=O_W[:, 5 * (s % 2) + 2, :],
                            op0=ALU.max, op1=ALU.add).then_inc(sb_l, 1)
                add_out("o_out", 192, 2)

            def route(l):
                w = lambda i: work[:, i, :]
                w8 = lambda i: work[:, i, 0:8]
                w2 = lambda i: work[:, i, 0:2]
                by_token = lambda ap: ap.rearrange("p (t e) -> p t e", t=TT)
                by_group = lambda ap: ap.rearrange("p (g e) -> p g e", e=4)
                per_token = lambda i, n: w2(i).unsqueeze(2).to_broadcast([P, TT, n])
                per_group = lambda i: w8(i).unsqueeze(2).to_broadcast([P, 8, 4])

                def step(instruction):
                    line(instruction)
                    line.wait()

                def first_best(dst, value, best, key, weights, n):
                    step(dve.tensor_reduce(w2(best), by_token(value), AX.X, ALU.max))
                    step(tt(by_token(key), by_token(value), per_token(best, n), ALU.is_equal))
                    step(tt(key, key, weights, ALU.mult))
                    step(dve.tensor_reduce(w2(best), by_token(key), AX.X, ALU.max))
                    step(tt(by_token(dst), by_token(key), per_token(best, n), ALU.is_equal))

                dve.wait_ge(ro_scores, l + 1)
                step(tt(w(1), w(0), router_b[:, :, :].rearrange("p t e -> p (t e)"), ALU.add))
                e = [by_group(w(1))[:, :, i] for i in range(4)]
                line(tt(w8(2), e[0], e[1], ALU.max))
                line(tt(w8(3), e[0], e[1], ALU.min))
                line(tt(w8(4), e[2], e[3], ALU.max))
                step(tt(w8(5), e[2], e[3], ALU.min))
                line(tt(w8(6), w8(2), w8(4), ALU.max))
                line(tt(w8(7), w8(2), w8(4), ALU.min))
                step(tt(w8(8), w8(3), w8(5), ALU.max))
                step(tt(w8(9), w8(7), w8(8), ALU.max))
                step(tt(w8(10), w8(6), w8(9), ALU.add))
                first_best(w8(11), w8(10), 12, w8(13), tab("w4"), 4)
                line(ts(w8(14), w8(11), BIG, -BIG, ALU.mult, ALU.add))
                step(tt(by_group(w(15)), by_group(w(1)), per_group(11), ALU.mult))
                step(tt(by_group(w(15)), by_group(w(15)), per_group(14), ALU.add))
                first_best(w(16), w(15), 12, w(17), tab("w16"), NE)
                step(stt(out=w(15), in0=w(16), scalar=-2.0 * BIG, in1=w(15), op0=ALU.mult, op1=ALU.add))
                first_best(w(18), w(15), 12, w(17), tab("w16"), NE)
                step(tt(w(16), w(16), w(18), ALU.add))
                step(tt(w(19), w(0), w(16), ALU.mult))
                step(dve.tensor_reduce(w2(20), by_token(w(19)), AX.X, ALU.add))
                step(dve.reciprocal(w2(21), w2(20)))
                tt(by_token(w(22)), by_token(w(19)), per_token(21, NE), ALU.mult).then_inc(ro_comb, 1)

            def moe(l):
                u0 = UNIT0[f"moe{l}"]
                route(l)

                def body(g, s, e):
                    for f in range(ET):
                        dve.wait_ge(mo_silu, e * 4 + (4 * NE * l + f + 1))
                        tt(SG[:, f, S:2 * S], SG[:, f, 0:S], row(CB, e), ALU.mult).then_inc(mo_weighted, 1)
                        dve.wait_ge(mo_weighted, e * 4 + (4 * NE * l + f + 1))
                        wait(dve, unit_done, e * 6 + (u0 - 6))
                        tt(G[:, 4 * s + f, 0:S], SG[:, f, S:2 * S], PS[:, f, S:2 * S], ALU.mult).then_inc(mo_g, 1)
                repeat(dve, NE, 2, body)
                dve.wait_ge(y_psum, l + 1)
                for d in range(KT):
                    stt(out=X[:, d, 0:S], in0=PS[:, 4 + d // 2, (d % 2) * S:(d % 2 + 1) * S],
                        scalar=mod_col(144 + 48 * l, 5, d, 0), in1=X[:, d, 0:S], op0=ALU.mult, op1=ALU.add)\
                        .then_inc(x_updated, 1)

            dve.wait_ge(ld_rest, REST)
            dve.tensor_copy(ext[:, 0:127], rel[:, 0:1].to_broadcast([8, 127])).then_inc(ext_ready, 1)
            dve.tensor_copy(ext[:, 127:319], rel[:, :]).then_inc(ext_ready, 1)
            dve.tensor_copy(ext[:, 319:512], rel[:, REL - 1:REL].to_broadcast([8, 193])).then_inc(ext_ready, 1)
            dve.wait_ge(ld_first, 32)
            take_mods(0, UNIT0["mod"] + 11)
            norm(0)
            up(0)
            take_mods(1, UNIT0["down0"] - 1)
            down(0)
            norm(1)
            mixer_a()
            norm(2)
            up(1)
            take_mods(2, UNIT0["down1"] - 1)
            down(1)
            norm(3)
            up(2)
            take_mods(3, UNIT0["down2"] - 1)
            down(2)
            norm(4)
            mixer_c()
            norm(5)
            up(3)
            take_mods(4, UNIT0["down3"] - 1)
            down(3)
            norm(6)
            mixer_e()
            norm(7)
            moe(0)
            norm(8)
            mixer_o()
            norm(9)
            moe(1)


def units_of(w):
    m = w.shape[-1]
    return w.reshape(KT, P, m // 256, 256).transpose(2, 1, 0, 3).reshape(m // 256, P, UW)


def pairs_of(gate, up):
    m = gate.shape[-1]
    both = np.stack([gate, up], 1).reshape(KT, P, 2, m // P, P)
    return both.transpose(3, 1, 0, 2, 4).reshape(m // P, P, UW)


def by_partition(v):
    return v.reshape(-1, P).T


def kernel(**inputs):
    import concourse.bacc as bacc
    from concourse.bass_utils import run_bass_kernel_spmd

    a = {k: np.ascontiguousarray(v) for k, v in inputs.items()}
    x_in = np.concatenate([a["x"][0], a["ctx"][0]], 0).T.reshape(KT, P, 2 * S).transpose(1, 0, 2)
    c = [by_partition(v) for v in (a["c"][0], a["c_ctx"], a["c_2"][0], a["c_2"][0])]
    cols = np.concatenate([
        np.stack(c, 2).reshape(P, -1),
        by_partition(np.concatenate([a["b_mod"].reshape(-1), a["ada_b_2"].reshape(-1)])),
        by_partition(np.concatenate([a["norm_g"].reshape(-1), a["norm1_g_2"].reshape(-1), a["norm2_g_2"].reshape(-1)])),
        by_partition(a["pool_scale"][0]), by_partition(a["v_norm_g"][0]),
        *(np.tile(v, 2)[:, None] for v in (a["qk_norm_g"][0, 0], a["qk_norm_g"][0, 1],
                                           a["att_q_norm_g_2"][0], a["att_k_norm_g_2"][0]))], 1)
    heads = np.concatenate([np.arange(h * 64, h * 64 + 64) for i in range(4) for h in (i, 4 + i)])
    w_in_a = a["w_in_a"][0]
    w_in_a = np.concatenate([w_in_a[:, heads], w_in_a[:, 512:]], 1)
    w_out_a = a["w_out_a"][0]
    w_out_a = np.concatenate([w_out_a[heads], w_out_a[512:]], 0)
    even = np.split(a["even_w_in_2"][0], 7, axis=1)
    even = np.concatenate([even[i] for i in (0, 1, 4, 5, 3, 2, 6)], 1)
    lin = np.concatenate([units_of(w) for w in (w_in_a, w_out_a, a["w_in_c"][0], a["w_out_c"][0], even,
                                                a["even_w_out_2"][0], a["odd_w_in_2"][0], a["odd_w_out_2"][0])])
    mod = np.concatenate([units_of(w) for w in (*a["w_mod"], *a["ada_w_2"])])
    w13 = a["ffn_w13"].reshape(4, D, 2 * FF)
    up = np.concatenate([pairs_of(w[:, :FF], w[:, FF:]) for w in w13])
    w2 = a["ffn_w2"].reshape(4, FT, P, KT, P)
    down = w2.transpose(0, 3, 2, 1, 4).reshape(4 * KT, P, FT * P)
    moe = np.empty((2, NE, 6, P, UW), np.float32)
    for l in range(2):
        for e in range(NE):
            moe[l, e, 0:4] = pairs_of(a["exp_w_gate_2"][l, e], a["exp_w_up_2"][l, e])
            moe[l, e, 4:6] = a["exp_w_down_2"][l, e].reshape(2, 2, P, D).transpose(0, 2, 1, 3).reshape(2, P, UW)
    arrays = {
        "x_in": x_in, "cols_in": cols, "tabs_in": tables(),
        "pool_w_in": a["pool_w"][0].transpose(1, 0, 2), "w_sp_in": a["w_sp"][0].transpose(2, 0, 1),
        "b_sp_in": np.broadcast_to(a["b_sp"][0][None], (P, 8, P)),
        "router_in": a["router_w_2"].reshape(KT, P, NE).transpose(1, 0, 2),
        "router_b_in": np.broadcast_to(a["router_b_2"], (P, TT, NE)),
        "rel_in": a["att_rel_bias_2"][0][:, ::-1],
        "mod_w": mod, "up_w": up, "down_w": down, "lin_w": lin, "moe_w": moe.reshape(-1, P, UW),
    }
    arrays = {k: np.ascontiguousarray(v) for k, v in arrays.items()}
    nc = bacc.Bacc("TRN2", target_bir_lowering=False, num_devices=1)
    aps = {k: nc.dram_tensor(k, v.shape, F32, kind="ExternalInput").ap() for k, v in arrays.items()}
    ext_dram = nc.dram_tensor("ext_dram", (8, 512), F32, kind="Internal").ap()
    out = nc.dram_tensor("out", (P, KT, S), F32, kind="ExternalOutput").ap()
    program(nc, ext_dram=ext_dram, out=out, **aps)
    got = run_bass_kernel_spmd(nc, [arrays], core_ids=[0]).results[0]["out"]
    return got.transpose(2, 1, 0).reshape(1, S, D)
```

```python
from contextlib import ExitStack

import numpy as np

import concourse.bass as bass
from concourse import mybir

ALU = mybir.AluOpType
ACT = mybir.ActivationFunctionType
AX = mybir.AxisListType
F32 = mybir.dt.float32

P = 128
D = 1024
KT = D // P
S = 256
TT = S // P
FF = 2816
FT = FF // P
GRID_W = 64
THETA = 10000.0
EPS = 1e-6
WINDOWS = (2, 4, 8, 16)
CH = 64
NE, NG, DE = 16, 4, 512
ET = DE // P
REL = 192
BIG = 1e30

UW = KT * 2 * P
CAP = 96
SLOTS = 4
BANK = 512
SQRT, EXP_LN = 3, 6

MOD_BASE = (0, 9 * KT, 18 * KT, 24 * KT)
MOD_TILES = 30 * KT

ROW_TILE0 = 5 * KT
ROW0 = (0, 15, 20)
N_ROWS = 25
N_ROWS_C = 13

UNITS = (
    ("mod", 12), ("up0", FT + 8), ("down0", KT), ("a_in", 5), ("a_out", 4),
    ("up1", FT), ("down1", KT), ("up2", FT), ("down2", KT), ("c_in", 8), ("c_out", 4),
    ("up3", FT), ("down3", KT), ("e_in", 14), ("e_out", 4), ("moe0", NE * 6),
    ("o_in", 12), ("o_out", 4), ("moe1", NE * 6),
)
UNIT0 = {}
_u = 0
for _name, _n in UNITS:
    UNIT0[_name] = _u
    _u += _n


def ups(f):
    u0 = UNIT0[f"up{f}"]
    if f == 3:
        return ((FT, 1, u0, 0, 0),)
    return ((20, 1, u0, 0, 3 if f == 0 else 1), (FT - 20, 5 if f == 0 else 1, u0 + 20, 20, 0))


def chunks(rows, s):
    if rows == 3:
        return [(s, k) for k in range(KT)] if s < 3 else []
    return [(0, k) for k in ((0, 1, 2), (3, 4, 5), (6, 7), ())[s]] if rows else []


LIN0 = {"a_in": 0, "a_out": 5, "c_in": 9, "c_out": 17, "e_in": 21, "e_out": 35, "o_in": 39, "o_out": 51}
HEAD0 = {"a": 0, "e": 3, "r": 7}
ROT0 = {"a": 0, "e": 3}
LIN_TILE0 = {"a_in": 0, "c_in": 6, "e_in": 14, "o_in": 28}
UPDATES = {"load": 0, "down0": 16, "a_out": 24, "down1": 32, "down2": 40, "c_out": 48, "down3": 56, "e_out": 64,
           "moe0": 72, "o_out": 80, "moe1": 88}

REST = 16 * 7

_COLS = (("c", KT * 4), ("mod_b", MOD_TILES), ("norm", 10 * KT), ("pool_scale", 4), ("v_gain", KT),
         ("q_gain", 1), ("k_gain", 1), ("aq_gain", 1), ("ak_gain", 1))
COL, _c = {}, 0
for _name, _n in _COLS:
    COL[_name] = slice(_c, _c + _n)
    _c += _n
NCOLS = _c

_TABS = (("ident", P), ("flip", P), ("mean64", P), ("mean128", P), ("mean1024", P), ("rot_axial", P),
         ("rot_half", P), ("upper", P), ("ones", P), ("zeros", P), ("w4", 8), ("w16", 32), ("iota", CAP),
         ("cos_axial", S), ("sin_axial", S), ("cos_half", S), ("sin_half", S),
         ("pool", 4 * TT * S), ("decay", 4 * TT * S), ("band", TT * S), ("before", 3 * P), ("after", 3 * P))
TAB, _c = {}, 0
for _name, _n in _TABS:
    TAB[_name] = slice(_c, _c + _n)
    _c += _n
NTABS = _c

NORMS = ((2 * S, 0, 0, 1, 0, "load"), (2 * S, 0, 3, 4, 1, "down0"), (S, 0, 6, 7, 2, "a_out"),
         (S, 72, 0, 1, 3, "down1"), (S, 72, 3, 4, 4, "down2"), (S, 72, 6, 7, 5, "c_out"),
         (S, 144, 0, 1, 6, "down3"), (S, 144, 3, 4, 8, "e_out"), (S, 192, 0, 1, 7, "moe0"),
         (S, 192, 3, 4, 9, "o_out"))
H_TILE0 = [0]
for _norm in NORMS:
    H_TILE0.append(H_TILE0[-1] + KT * _norm[0] // S)
FFNS = ((0, 0, 2), (2, 0, 8), (3, 72, 2), (5, 72, 8))
MOD_RUNS = ((0, 24), (24, ROW_TILE0))


def tables():
    t = {}
    i = np.arange(P)
    t["ident"] = np.eye(P)
    t["flip"] = np.eye(P)[::-1]
    t["mean64"] = (i[:, None] // 64 == i[None, :] // 64) / 64.0
    t["mean128"] = np.full((P, P), 1.0 / P)
    t["mean1024"] = np.full((P, P), 1.0 / D)
    def partner(width):
        r = np.zeros((P, P))
        for m in range(P):
            a = m % width
            if a < width // 2:
                r[m + width // 2, m] = -1.0
            else:
                r[m - width // 2, m] = 1.0
        return r
    t["rot_axial"], t["rot_half"] = partner(32), partner(P)
    t["upper"] = (i[:, None] >= i[None, :])
    t["ones"] = np.ones((P, P))
    t["zeros"] = np.zeros((P, P))
    t["w4"] = np.tile([4.0, 3.0, 2.0, 1.0], (P, 2))
    t["w16"] = np.tile(np.arange(16, 0, -1.0), (P, 2))
    t["iota"] = np.tile(np.arange(float(CAP)), (P, 1))
    n = np.arange(S)
    inv = THETA ** (-np.arange(0, 32, 2) / 32.0)
    where = np.where((i % 64)[:, None] < 32, n[None, :] // GRID_W, n[None, :] % GRID_W)
    angle = where * inv[i % 16][:, None]
    t["cos_axial"], t["sin_axial"] = np.cos(angle), np.sin(angle)
    inv = THETA ** (-np.arange(0, P, 2) / float(P))
    angle = n[None, :] * inv[i % 64][:, None]
    t["cos_half"], t["sin_half"] = np.cos(angle), np.sin(angle)
    pool = np.zeros((P, 4, TT, S))
    for g, w in enumerate(WINDOWS):
        lo, hi = np.clip(n - w // 2, 0, S), np.clip(n + w // 2, 0, S)
        m = ((n[:, None] >= lo) & (n[:, None] < hi)) / (hi - lo) - np.eye(S)
        pool[:, g] = m.reshape(TT, P, S).transpose(1, 0, 2)
    t["pool"] = pool
    gamma = 1.0 - 2.0 ** (-5.0 - np.arange(4))
    d = np.abs(n[:, None] - n[None, :])
    seen = n[:, None] // CH <= n[None, :] // CH
    decay = np.stack([np.where(seen, g ** d, 0.0) * P ** -0.5 for g in gamma])
    t["decay"] = decay.reshape(4, TT, P, S).transpose(2, 0, 1, 3)
    band = np.where(n[None, :] // CH <= n[:, None] // CH, 0.0, -BIG)
    t["band"] = band.reshape(TT, P, S).transpose(1, 0, 2)
    strict = (i[:, None] < i[None, :]).astype(float)
    before = np.concatenate([strict, np.ones((P, P)), strict], 1)
    t["before"], t["after"] = before, (before - 1.0) * BIG
    return np.concatenate([np.asarray(t[k], np.float32).reshape(P, n) for k, n in _TABS], 1)


class Line:

    def __init__(self, eng, sem):
        self.eng, self.sem, self.n = eng, sem, 0

    def __call__(self, instruction):
        instruction.then_inc(self.sem, 1)
        self.n += 1

    def wait(self):
        self.eng.wait_ge(self.sem, self.n)


def repeat(eng, n, step, body, peel=0, tail=0):
    whole = n // step
    first, end = peel, whole - tail
    if end - first < 2:
        first = end = whole
    for g in range(first):
        for s in range(step):
            body(g, s, g * step + s)
    if first < end:
        with eng.Fori(first, end) as g:
            for s in range(step):
                body(g, s, g * step + s)
    for i in range(end * step, n):
        body(i // step, i % step, i)


def wait(eng, sem, value):
    if not isinstance(value, int) or value > 0:
        eng.wait_ge(sem, value)


def row(ap, i):
    return ap[:, bass.ds(i, 1), :].rearrange("p a n -> p (a n)")


def program(nc, x_in, cols_in, tabs_in, pool_w_in, w_sp_in, b_sp_in, router_in, router_b_in, rel_in,
            mod_w, mod_rows, up_w, down_w, lin_w, moe_w, ext_dram, out):
    with ExitStack() as ctx:
        def sb(name, shape):
            return ctx.enter_context(nc.sbuf_tensor(name, shape, F32))

        def sem(name):
            return ctx.enter_context(nc.semaphore(name))

        ring = sb("ring", [P, SLOTS, FT * P])
        X = sb("X", [P, KT, 2 * S])
        H = sb("H", [P, KT, 2 * S])
        G = sb("G", [P, FT, 2 * S])
        SG = sb("SG", [P, 4, BANK])
        CAT = sb("CAT", [P, KT, S])
        CB = sb("CB", [P, NE, S])
        cols = sb("cols", [P, NCOLS])
        tabs = sb("tabs", [P, NTABS])
        pool_w = sb("pool_w", [P, 4, P])
        w_sp = sb("w_sp", [P, 8, P])
        b_sp = sb("b_sp", [P, 8, P])
        router_w = sb("router_w", [P, KT, NE])
        router_b = sb("router_b", [P, TT, NE])
        rel, ext = H[0:8, 1, 0:REL], H[0:8, 0, :]
        cond = sb("cond", [P, KT, 4])
        M = sb("M", [P, MOD_TILES, 2])
        NA = sb("NA", [P, 10, 2, KT])
        HG = sb("HG", [P, 4 * 2 * KT])
        roots = sb("roots", [P, 2, 2 * S])
        rt, rs = roots[:, 0, :], roots[:, 1, :]
        cond_rows = sb("cond_rows", [P, N_ROWS, KT])
        over = ctx.enter_context(nc.sbuf_tensor("over", [1, 1], mybir.dt.int32))
        small = sb("small", [P, 64])
        eps = sb("eps", [P, 1])
        work = sb("work", [P, 24, 32])
        combT = rs[0:NE, 0:S]
        PS = ctx.enter_context(nc.psum_tensor("PS", [P, 8, BANK], F32))

        full = [sem(f"weights_full{s}") for s in range(SLOTS)]
        unit_done = sem("unit_done")
        ld_first, ld_rest, ld_ext = sem("ld_first"), sem("ld_rest"), sem("ld_ext")
        ext_ready, ext_stored = sem("ext_ready"), sem("ext_stored")
        act_line, dve_line = sem("act_line"), sem("dve_line")
        cond_ready, mods_ready = sem("cond_ready"), sem("mods_ready")
        rows_full = [sem(f"rows_full{k}") for k in range(4)]
        acc_steps, colsum_done, rows_taken = sem("acc_steps"), sem("colsum_done"), sem("rows_taken")
        sq_ready, ms_psum, rt_ready, xn_ready, h_ready = (
            sem(n) for n in ("sq_ready", "ms_psum", "rt_ready", "xn_ready", "h_ready"))
        silu_ready, g_ready, x_updated = sem("silu_ready"), sem("g_ready"), sem("x_updated")
        lin_ready = sem("lin_ready")
        hsq_ready, hms_psum, hrt_ready, hn_ready = (
            sem(n) for n in ("hsq_ready", "hms_psum", "hrt_ready", "hn_ready"))
        rot_psum, rot_ready = sem("rot_psum"), sem("rot_ready")
        pool_psum, pool_ready, poolw_psum = sem("pool_psum"), sem("pool_ready"), sem("poolw_psum")
        at_scores, at_max, at_exp, at_probs, at_tpsum, at_tready, at_out, at_kept = (
            sem(n) for n in ("at_scores", "at_max", "at_exp", "at_probs", "at_tpsum", "at_tready",
                             "at_out", "at_kept"))
        cat_ready = sem("cat_ready")
        v_sums, v_ready, sv_psum = sem("v_sums"), sem("v_ready"), sem("sv_psum")
        re_scores, re_decayed, re_out, re_kept = (
            sem(n) for n in ("re_scores", "re_decayed", "re_out", "re_kept"))
        sb_scores, sb_z, sb_zs, sb_log, sb_l, sb_lm, sb_sums, sb_w, sb_a, sb_out, sb_kept = (
            sem(n) for n in ("sb_scores", "sb_z", "sb_zs", "sb_log", "sb_l", "sb_lm", "sb_sums", "sb_w",
                             "sb_a", "sb_out", "sb_kept"))
        ro_psum, ro_scores, ro_masks, ro_ranks, ro_listed = (
            sem(n) for n in ("ro_psum", "ro_scores", "ro_masks", "ro_ranks", "ro_listed"))
        ht_psum, ht_ready = sem("ht_psum"), sem("ht_ready")
        mo_sel, mo_gpsum, mo_gathered, mo_tpsum, mo_tready, mo_silu, mo_g, mo_y, mo_scattered = (
            sem(n) for n in ("mo_sel", "mo_gpsum", "mo_gathered", "mo_tpsum", "mo_tready", "mo_silu",
                             "mo_g", "mo_y", "mo_scattered"))
        y_psum = sem("y_psum")
        rest = [{n: sem(f"rest{l}_{n}") for n in ("full0", "full1", "full2", "full3", "unit", "tpsum", "t",
                                                  "bpsum", "b", "silu", "weighted", "g")} for l in range(2)]
        stored, eps_ready = sem("stored"), sem("eps_ready")

        def tab(name):
            return tabs[:, TAB[name]]

        def col(name):
            return cols[:, COL[name]]

        def mod_col(base, m, d, j):
            at = base + m * KT + d
            return M[:, at, j:j + 1]

        def slot(u, k=KT):
            return ring[:, u % SLOTS, 0:UW].rearrange("p (k c) -> p k c", k=k)

        g_flat = G[:, :, :].rearrange("p a b -> p (a b)")

        def scratch(at, *shape):
            n = int(np.prod(shape))
            v = g_flat[:, at:at + n]
            if len(shape) == 1:
                return v
            if len(shape) == 2:
                return v.rearrange("p (a b) -> p a b", a=shape[0])
            return v.rearrange("p (a b c) -> p a b c", a=shape[0], b=shape[1])

        A_QK, A_SQ, A_R = scratch(0, 1536), scratch(1536, 1536), scratch(3072, 1536)
        A_V, A_P, A_POOLED = scratch(4608, 4, P), scratch(5120, TT, 512), scratch(6144, 4, S)
        PROBS, PT = scratch(7168, 4, 512), scratch(9216, 2, 512)
        C_U, C_V, C_T = scratch(0, 8, S), scratch(2048, TT, D), scratch(4096, 8, S)
        C_SQ = scratch(6144, TT, D)
        E_QK, E_G = scratch(0, 4096), scratch(4096, 1024)
        E_V = scratch(5120, TT, 1024)
        E_T, E_R = scratch(7168, 2048), scratch(9216, 2048)
        HANKEL = CB[:, 0:12, :].rearrange("p a b -> p (a b)").rearrange("p (h n) -> p h n", h=8)
        ROWS_W = CB[:, :, :].rearrange("p a b -> p (a b)").rearrange("p (k n) -> p k n", k=4)
        cat_flat = CAT[:, :, :].rearrange("p a b -> p (a b)")
        ACC = (cat_flat[:, 0:D], cat_flat[:, D:2 * D], roots[:, :, :].rearrange("p a b -> p (a b)"))
        H_TOK = cat_flat.rearrange("p (t d) -> p t d", t=TT)
        HX, SWT = scratch(0, 2, KT * CAP), scratch(1536, 2, S)
        SEL, SELW = scratch(2048, 2, TT, CAP), scratch(2432, 2, TT, CAP)
        GX, YG = scratch(2816, 2, ET, CAP), scratch(3584, D)
        O_QK, O_V = scratch(0, 16, S), scratch(4096, TT, D)
        O_W = scratch(6144, 11, 384)

        def o_work(what, h):
            first, n = {"z": (0, 2), "zs": (2, 3), "log": (5, 2), "lm": (7, 2), "a": (9, 2)}[what]
            return O_W[:, first + h % n, :]

        def squares(n, d):
            N, before = NORMS[n][0], NORMS[n][5]
            if not before.startswith("down"):
                return G[:, d, 0:N]
            return CAT[:, d, :] if N == S else SG[:, d, :] if d < 4 else cat_flat[:, (d - 4) * N:(d - 3) * N]

        def mean_squares(n):
            return PS[:, 0 if NORMS[n][5].startswith("moe") else 7, 0:NORMS[n][0]]

        block = ctx.enter_context(nc.Block())

        @block.sync
        def _(sp):
            def load(u, g, turns, count, width, src):
                wait(sp, unit_done, count - SLOTS)
                sp.dma_start(ring[:, u % SLOTS, 0:width], src).then_inc(full[u % SLOTS], 16)

            def source(w, i):
                return w[bass.ds(i, 1)].rearrange("a p n -> p (a n)")

            def stream(name, n, w, first, width=UW, peel=0):
                u0 = UNIT0[name]
                repeat(sp, n, SLOTS, lambda g, s, i: load(u0 + s, g, 1, i + (u0 + 1), width,
                                                          source(w, i + first)), peel)

            def up(f):
                for n, stride, u0, j0, rows in ups(f):
                    lead = 2 if rows else 0
                    for i in range(lead):
                        load(u0 + i, 0, 0, u0 + i + 1, UW, source(up_w, FT * f + j0 + i))

                    def body(g, s, i):
                        if not (isinstance(i, int) and i + lead >= n):
                            load(u0 + lead + s * stride, g, 0, i * stride + (u0 + lead + 1), UW,
                                 source(up_w, i + (FT * f + j0 + lead)))
                        for k in range(1, stride):
                            load(u0 + s * stride + k, g, 0, i * stride + (u0 + k + 1), UW,
                                 source(mod_w, i * 4 + (12 + k - 1)))
                        for r, k in chunks(rows, s):
                            q = g * (KT * rows) + (KT * (ROW0[f] + r) + k)
                            wait(sp, acc_steps, q - 3)
                            sp.dma_start(ROWS_W[:, k % 4, :], source(mod_rows, q)).then_inc(rows_full[k % 4], 16)
                    repeat(sp, n, 4, body, peel=(1 if f == 0 else 0), tail=(1 if rows else 0))

            def down(f):
                stream(f"down{f}", KT, down_w, KT * f, FT * P)

            def rest_pass(l):
                sems = rest[l]
                u0 = UNIT0[f"moe{l}"]
                sp.wait_ge(ro_listed, l + 1)
                with sp.If(sp.value_load(over[0:1, 0:1], min_val=0, max_val=1) > 0):
                    sp.wait_ge(unit_done, u0 + NE * 6)

                    def body(g, s, i):
                        wait(sp, sems["unit"], i - 3)
                        sp.dma_start(ring[:, s, 0:UW], source(moe_w, i + NE * 6 * l)).then_inc(sems[f"full{s}"], 16)
                    repeat(sp, NE * 6, SLOTS, body, peel=1)
                    sp.wait_ge(sems["unit"], NE * 6)

            stream("mod", 12, mod_w, 0, peel=1)
            up(0)
            down(0)
            stream("a_in", 5, lin_w, LIN0["a_in"])
            stream("a_out", 4, lin_w, LIN0["a_out"])
            up(1)
            down(1)
            up(2)
            down(2)
            stream("c_in", 8, lin_w, LIN0["c_in"])
            stream("c_out", 4, lin_w, LIN0["c_out"])
            up(3)
            down(3)
            stream("e_in", 14, lin_w, LIN0["e_in"])
            stream("e_out", 4, lin_w, LIN0["e_out"])
            stream("moe0", NE * 6, moe_w, 0)
            rest_pass(0)
            stream("o_in", 12, lin_w, LIN0["o_in"])
            stream("o_out", 4, lin_w, LIN0["o_out"])
            stream("moe1", NE * 6, moe_w, NE * 6)
            rest_pass(1)
            sp.wait_ge(x_updated, UPDATES["moe1"])
            sp.dma_start(out, X[:, :, 0:S]).then_inc(stored, 16)
            sp.wait_ge(stored, 16)

        @block.tensor
        def _(pe):
            mm, tr = pe.matmul, pe.transpose

            def arrived(u, g=0, turns=0):
                pe.wait_ge(full[u % SLOTS], g * (16 * turns) + 16 * (u // SLOTS + 1))

            def mod_unit(u, ct):
                w = slot(u)
                for c in range(2):
                    for k in range(KT):
                        last = mm(PS[:, 6, 2 * (ct + c):2 * (ct + c) + 2], w[:, k, c * P:(c + 1) * P],
                                  cond[:, k, 0:2], start=(k == 0), stop=(k == KT - 1))
                last.then_inc(unit_done, 1)

            def first_mods():
                u0 = UNIT0["mod"]
                pe.wait_ge(cond_ready, 1)
                for i in range(12):
                    arrived(u0 + i)
                    mod_unit(u0 + i, 2 * i)

            def column_sums(r, bank, acc, taken):
                pe.wait_ge(acc_steps, r * KT + KT)
                wait(pe, rows_taken, taken)
                for d in range(KT):
                    last = mm(PS[:, bank, d:d + 1], ACC[acc][:, d * P:(d + 1) * P], tab("ones")[:, 0:1],
                              start=True, stop=True)
                last.then_inc(colsum_done, 1)

            def h_arrived(n, k):
                pe.wait_ge(h_ready, H_TILE0[n] + (k + 1) * (NORMS[n][0] // S))

            def norm(n):
                N = NORMS[n][0]
                for d in range(KT):
                    pe.wait_ge(sq_ready, KT * n + d + 1)
                    last = mm(mean_squares(n), tab("mean1024"), squares(n, d), start=(d == 0), stop=(d == KT - 1))
                last.then_inc(ms_psum, 1)

            def up(f):
                N = NORMS[FFNS[f][0]][0]
                depth = 2 if N > S else 4
                pe.wait_ge(mods_ready, min(f + 1, 2))
                for n, stride, u0, j0, rows in ups(f):
                    turns = 4 * stride // SLOTS

                    def body(g, s, i):
                        u = u0 + s * stride
                        arrived(u, g, turns)
                        wait(pe, g_ready, i + (FT * f + j0 - depth + 1))
                        w = slot(u)
                        for h in range(2):
                            dst = PS[:, 2 * (s % 2) + h, :] if N > S else PS[:, s % 4, h * S:(h + 1) * S]
                            for k in range(KT):
                                if u == UNIT0[f"up{f}"] and isinstance(i, int) and h == 0:
                                    h_arrived(FFNS[f][0], k)
                                last = mm(dst, w[:, k, h * P:(h + 1) * P], H[:, k, 0:N],
                                          start=(k == 0), stop=(k == KT - 1))
                        last.then_inc(unit_done, 1)
                        for k in range(1, stride):
                            arrived(u + k)
                            mod_unit(u + k, 24 + 2 * (4 * i + k - 1))
                        if rows == 3 and s >= 1:
                            r = g * 3 + (ROW0[f] + s - 1)
                            column_sums(r, (4, 5, 7)[s - 1], s - 1, r - 2)
                        if rows == 1 and s == 3:
                            r = g + ROW0[f]
                            column_sums(r, 4, 0, r)
                    repeat(pe, n, 4, body, peel=1)

            def down(f):
                N = NORMS[FFNS[f][0]][0]
                sides, u0 = N // S, UNIT0[f"down{f}"]
                before = UPDATES[f"down{f}"] - sides * KT
                pe.wait_ge(g_ready, FT * (f + 1))

                def body(g, s, i):
                    arrived(u0 + s, g, 1)
                    wait(pe, x_updated, i * sides + (before - 3 * sides))
                    for j in range(FT):
                        last = mm(PS[:, s, 0:N], ring[:, (u0 + s) % SLOTS, j * P:(j + 1) * P], G[:, j, 0:N],
                                  start=(j == 0), stop=(j == FT - 1))
                    last.then_inc(unit_done, 1)
                repeat(pe, KT, SLOTS, body, peel=(2 if f == 0 else 0))

            def by_features(name, n, unit, tile, after):
                u0, t0 = UNIT0[name] + unit, LIN_TILE0[name] + tile

                def body(g, s, i):
                    arrived(u0 + s, g, 1)
                    wait(pe, lin_ready, i + (t0 - 3))
                    w = slot(u0 + s)
                    for c in range(2):
                        for k in range(KT):
                            if isinstance(i, int) and i == 0 and c == 0:
                                h_arrived(after, k)
                            last = mm(PS[:, (tile + s) % 4, c * S:(c + 1) * S], w[:, k, c * P:(c + 1) * P],
                                      H[:, k, 0:S], start=(k == 0), stop=(k == KT - 1))
                    last.then_inc(unit_done, 1)
                repeat(pe, n, SLOTS, body, peel=1)

            def by_tokens(name, n, unit, tile):
                u0, t0 = UNIT0[name] + unit, LIN_TILE0[name] + tile

                def body(g, s, i):
                    arrived(u0 + s, g, 1)
                    wait(pe, lin_ready, i + (t0 - 3))
                    w = slot(u0 + s)
                    for t in range(TT):
                        for k in range(KT):
                            last = mm(PS[:, (tile + s) % 4, t * S:(t + 1) * S], H[:, k, t * P:(t + 1) * P],
                                      w[:, k, :], start=(k == 0), stop=(k == KT - 1))
                    last.then_inc(unit_done, 1)
                repeat(pe, n, SLOTS, body)

            def out_proj(name):
                u0 = UNIT0[name]
                for i in range(4):
                    arrived(u0 + i)
                    w = slot(u0 + i)
                    for c in range(2):
                        for k in range(KT):
                            last = mm(PS[:, i, c * S:(c + 1) * S], w[:, k, c * P:(c + 1) * P], CAT[:, k, :],
                                      start=(k == 0), stop=(k == KT - 1))
                    last.then_inc(unit_done, 1)

            def head_norm(which, sq, n, mean):
                for c in range(n):
                    pe.wait_ge(hsq_ready, HEAD0[which] + c + 1)
                    mm(PS[:, c, :], tab(mean), sq[:, c * BANK:(c + 1) * BANK], start=True, stop=True)\
                        .then_inc(hms_psum, 1)

            def rotation(src, width, rot):
                for c in range(0, width, BANK):
                    n = min(BANK, width - c)
                    mm(PS[:, c // BANK, 0:n], tab(rot), src[:, c:c + n], start=True, stop=True)\
                        .then_inc(rot_psum, 1)

            def attention(which):
                first = 0 if which == "a" else 16
                keys = 4 if which == "a" else 2
                for s in range(19):
                    if s < 16:
                        i, half, t = s // 4, s // 2 % 2, s % 2
                        rows = slice(64 * half, 64 * half + 64)
                        if s >= 4:
                            pe.wait_ge(at_exp if which == "a" else at_max, first + s - 3)
                        if which == "a":
                            mm(PS[:, s % 4, :], A_QK[rows, i * S + t * P:i * S + t * P + P],
                               A_QK[rows, 4 * S:6 * S], start=True, stop=True).then_inc(at_scores, 1)
                        else:
                            q0 = 2048 + i * S + t * P
                            mm(PS[:, s % 4, 0:S], E_QK[rows, q0:q0 + P],
                               E_QK[rows, 3072 + i * S:3072 + (i + 1) * S], start=True, stop=False)
                            mm(PS[:, s % 4, 0:S], tab("flip"), HANKEL[:, 2 * i + half, P - P * t:P - P * t + S],
                               start=False, stop=True).then_inc(at_scores, 1)
                    if 2 <= s <= 17:
                        it = s - 2
                        pe.wait_ge(at_probs, first + it + 1)
                        if it >= 2:
                            pe.wait_ge(at_tready, first + it - 1)
                        for k in range(keys):
                            last = tr(PS[:, 4 + it % 2, k * P:(k + 1) * P], PROBS[:, it % 4, k * P:(k + 1) * P],
                                      tab("ident"))
                        last.then_inc(at_tpsum, 1)
                    if s >= 3:
                        it = s - 3
                        i, half, t = it // 4, it // 2 % 2, it % 2
                        pe.wait_ge(at_tready, first + it + 1)
                        if it % 4 == 0 and i >= 2:
                            pe.wait_ge(at_kept, first // 4 + i - 1)
                        for k in range(keys):
                            if which == "a":
                                v = A_V[:, k, 64 * half:64 * half + 64]
                            else:
                                v = E_V[:, k, 512 + (2 * i + half) * 64:512 + (2 * i + half) * 64 + 64]
                            last = mm(PS[64 * half:64 * half + 64, 6 + i % 2, t * P:(t + 1) * P], v,
                                      PT[:, it % 2, k * P:(k + 1) * P], start=(k == 0), stop=(k == keys - 1))
                        last.then_inc(at_out, 1)

            def mixer_a():
                u0 = UNIT0["a_in"]
                by_features("a_in", 2, 0, 0, 1)
                arrived(u0 + 2)
                w = slot(u0 + 2)
                for k in range(KT):
                    mm(PS[:, 2, :], w[:, k, 0:P], H[:, k, :], start=(k == 0), stop=(k == KT - 1))
                for t in range(2 * TT):
                    for k in range(KT):
                        last = mm(PS[:, 3, t * P:(t + 1) * P], H[:, k, t * P:(t + 1) * P], w[:, k, P:2 * P],
                                  start=(k == 0), stop=(k == KT - 1))
                last.then_inc(unit_done, 1)
                by_tokens("a_in", 2, 3, 4)
                head_norm("a", A_SQ, 3, "mean64")
                for g in range(4):
                    for t in range(TT):
                        last = mm(PS[:, 4 + g // 2, (g % 2) * S:(g % 2 + 1) * S], A_P[:, t, g * P:(g + 1) * P],
                                  tab("pool").rearrange("p (g t n) -> p g t n", g=4, t=TT)[:, g, t, :],
                                  start=(t == 0), stop=(t == TT - 1))
                last.then_inc(pool_psum, 1)
                pe.wait_ge(pool_ready, 2)
                for g in range(4):
                    last = mm(PS[:, 6 + g // 2, (g % 2) * S:(g % 2 + 1) * S], pool_w[:, g, :], A_POOLED[:, g, :],
                              start=True, stop=True)
                last.then_inc(poolw_psum, 1)
                pe.wait_ge(hn_ready, 3)
                rotation(A_QK, 5 * S, "rot_axial")
                pe.wait_ge(rot_ready, 3)
                pe.wait_ge(cat_ready, 1)
                attention("a")
                pe.wait_ge(at_kept, 4)
                out_proj("a_out")

            def mixer_c():
                by_features("c_in", 4, 0, 0, 4)
                by_tokens("c_in", 4, 4, 4)
                pe.wait_ge(v_ready, 2)
                for g in range(8):
                    for t in range(TT):
                        last = mm(PS[:, 4 + g // 2, (g % 2) * S + t * P:(g % 2) * S + (t + 1) * P],
                                  C_V[:, t, g * P:(g + 1) * P], w_sp[:, g, :], start=True, stop=True)
                    if g % 2:
                        last.then_inc(sv_psum, 1)
                pe.wait_ge(cat_ready, 2)
                out_proj("c_out")

            def mixer_e():
                by_features("e_in", 10, 0, 0, 6)
                by_tokens("e_in", 4, 10, 10)
                pe.wait_ge(lin_ready, LIN_TILE0["e_in"] + 14)
                rotation(E_QK, 2048, "rot_half")
                pe.wait_ge(rot_ready, 7)
                head_norm("e", E_T, 4, "mean64")
                pe.wait_ge(hrt_ready, HEAD0["e"] + 4)
                for h in range(4):
                    for t in range(TT):
                        last = mm(PS[:, h, t * S:(t + 1) * S], E_QK[:, 1024 + h * S + t * P:1024 + h * S + (t + 1) * P],
                                  E_QK[:, h * S:(h + 1) * S], start=True, stop=True)
                    last.then_inc(re_scores, 1)
                for h in range(4):
                    pe.wait_ge(re_decayed, h + 1)
                    for t in range(TT):
                        last = mm(PS[:, 4 + h // 2, (h % 2) * S:(h % 2 + 1) * S], E_V[:, t, h * P:(h + 1) * P],
                                  SG[:, h, t * S:(t + 1) * S], start=(t == 0), stop=(t == TT - 1))
                    last.then_inc(re_out, 1)
                head_norm("r", E_T[:, 1024:2048], 2, "mean128")
                pe.wait_ge(cat_ready, 4)
                pe.wait_ge(ld_ext, 16)
                attention("e")
                pe.wait_ge(at_kept, 8)
                out_proj("e_out")

            def mixer_o():
                by_features("o_in", 8, 0, 0, 8)
                by_tokens("o_in", 4, 8, 8)
                pe.wait_ge(lin_ready, LIN_TILE0["o_in"] + 12)
                for s in range(19):
                    if s < 16:
                        h, rows, tile = s, slice(64 * (s % 2), 64 * (s % 2) + 64), s // 2
                        q, k = O_QK[rows, tile, :], O_QK[rows, 8 + tile, :]
                        if h >= 2:
                            pe.wait_ge(sb_z, h - 1)
                        mm(PS[:, h % 2, 0:S], k[:, 0:P], q, start=True, stop=True)
                        mm(PS[:, h % 2, S:S + P], k[:, P:S], q[:, P:S], start=True, stop=True)\
                            .then_inc(sb_scores, 1)
                    if 1 <= s <= 16:
                        h = s - 1
                        lm = o_work("lm", h)
                        pe.wait_ge(sb_lm, h + 1)
                        if h >= 2:
                            pe.wait_ge(sb_w, h - 1)
                        mm(PS[:, 2 + h % 2, 0:S], tab("upper"), lm[:, 0:S], start=True, stop=False)
                        mm(PS[:, 2 + h % 2, P:S], tab("ones"), lm[:, S:S + P], start=False, stop=True)
                        mm(PS[:, 2 + h % 2, S:S + P], tab("upper"), lm[:, S:S + P], start=True, stop=True)\
                            .then_inc(sb_sums, 1)
                    if s >= 3:
                        h = s - 3
                        rows, tile = slice(64 * (h % 2), 64 * (h % 2) + 64), h // 2
                        a = o_work("a", h)
                        pe.wait_ge(sb_a, h + 1)
                        if h % 2 == 0 and tile >= 2:
                            pe.wait_ge(sb_kept, tile - 1)
                        mm(PS[rows, 4 + tile % 2, 0:S], O_V[:, 0, 64 * h:64 * h + 64], a[:, 0:S],
                           start=True, stop=False)
                        mm(PS[rows, 4 + tile % 2, P:S], O_V[:, 1, 64 * h:64 * h + 64], a[:, S:S + P],
                           start=False, stop=True).then_inc(sb_out, 1)
                pe.wait_ge(sb_kept, 8)
                out_proj("o_out")

            def moe(l):
                u0, e0 = UNIT0[f"moe{l}"], NE * l
                mask = work[:, 16, :].rearrange("p (t e) -> p t e", t=TT)
                for t in range(TT):
                    for k in range(KT):
                        if t == 0:
                            h_arrived(7 + 2 * l, k)
                        last = mm(PS[:, 0, t * NE:(t + 1) * NE], H[:, k, t * P:(t + 1) * P], router_w[:, k, :],
                                  start=(k == 0), stop=(k == KT - 1))
                last.then_inc(ro_psum, 1)
                for c in range(4):
                    t, half = c // 2, c % 2
                    for d in range(4):
                        last = tr(PS[:, 4 + c, d * P:(d + 1) * P], H[:, 4 * half + d, t * P:(t + 1) * P], tab("ident"))
                    last.then_inc(ht_psum, 1)
                pe.wait_ge(ro_masks, l + 1)
                mm(PS[:, 1, 0:NE], tab("before")[:, 0:P], mask[:, 0, :], start=True, stop=True)
                mm(PS[:, 1, NE:2 * NE], tab("before")[:, 0:P], mask[:, 1, :], start=True, stop=False)
                mm(PS[:, 1, NE:2 * NE], tab("ones"), mask[:, 0, :], start=False, stop=True)
                mm(PS[:, 1, 2 * NE:3 * NE], tab("ones"), mask[:, 0, :], start=True, stop=False)
                mm(PS[:, 1, 2 * NE:3 * NE], tab("ones"), mask[:, 1, :], start=False, stop=True)\
                    .then_inc(ro_ranks, 1)
                pe.wait_ge(ht_ready, 4 * (l + 1))
                for b in range(4):
                    mm(PS[:, 4 + b, :], tab("zeros"), tabs[:, 0:BANK], start=True, stop=False, skip_group_check=True)

                def gather(e, p):
                    pe.wait_ge(mo_sel, e + (e0 + 1))
                    for t in range(TT):
                        last = tr(PS[0:CAP, 2, t * P:(t + 1) * P], SELW[:, p, t, :], tab("ident"))
                    last.then_inc(mo_tpsum, 1)
                    wait(pe, mo_y, e * 2 + (2 * e0 - 2))
                    for b in range(2):
                        for d in range(4):
                            for t in range(TT):
                                last = mm(PS[:, b, d * CAP:(d + 1) * CAP], H_TOK[:, t, (4 * b + d) * P:(4 * b + d + 1) * P],
                                          SEL[:, p, t, :], start=(t == 0), stop=(t == TT - 1))
                        last.then_inc(mo_gpsum, 1)

                def scatter(e, p):
                    pe.wait_ge(mo_y, e * 2 + (2 * e0 + 2))
                    pe.wait_ge(mo_tready, e + (e0 + 1))
                    for d in range(KT):
                        last = mm(PS[:, 4 + d // 2, (d % 2) * S:(d % 2 + 1) * S], YG[0:CAP, d * P:(d + 1) * P],
                                  SWT[0:CAP, p, :], start=False, stop=False, skip_group_check=True)
                    last.then_inc(mo_scattered, 1)

                def body(g, s, e):
                    for f in range(ET):
                        u = u0 + 6 * s + f
                        arrived(u, g, 3)
                        wait(pe, mo_g, e * 4 + (4 * e0 + f - 1))
                        if f == 0:
                            pe.wait_ge(mo_gathered, e * 2 + (2 * e0 + 2))
                            pe.wait_ge(mo_tready, e + (e0 + 1))
                        if f == 2 and not (isinstance(e, int) and e == NE - 1):
                            pe.wait_ge(mo_tready, e + (e0 + 2))
                        w = slot(u)
                        for h in range(2):
                            for k in range(KT):
                                last = mm(PS[:, 2 + f % 2, h * CAP:(h + 1) * CAP], w[:, k, h * P:(h + 1) * P],
                                          HX[:, s, k * CAP:(k + 1) * CAP], start=(k == 0), stop=(k == KT - 1))
                        last.then_inc(unit_done, 1)
                        if f == 0 and not (isinstance(e, int) and e == 0):
                            scatter(e - 1, 1 - s)
                        if f == 1 and not (isinstance(e, int) and e == NE - 1):
                            pe.wait_ge(mo_g, e * 4 + (4 * e0 + 1))
                            gather(e + 1, 1 - s)
                    if not (isinstance(e, int) and e == NE - 1):
                        pe.wait_ge(mo_gathered, e * 2 + (2 * e0 + 4))
                    for h in range(2):
                        u = u0 + 6 * s + 4 + h
                        arrived(u, g, 3)
                        pe.wait_ge(mo_g, e * 4 + (4 * e0 + 2 * h + 2))
                        for f in range(2):
                            for n in range(2):
                                last = mm(PS[0:CAP, n, :], GX[:, s, 2 * h + f, :],
                                          ring[:, u % SLOTS, f * D + n * BANK:f * D + (n + 1) * BANK],
                                          start=(h + f == 0), stop=(h + f == 2), skip_group_check=True)
                        last.then_inc(unit_done, 1)

                gather(0, 0)
                repeat(pe, NE, 2, body, peel=1, tail=1)
                scatter(NE - 1, 1)
                rest_pass(l)
                for b in range(4):
                    last = mm(PS[:, 4 + b, :], tab("zeros"), tabs[:, 0:BANK], start=False, stop=True,
                              skip_group_check=True)
                last.then_inc(y_psum, 1)

            def rest_pass(l):
                sems = rest[l]
                with pe.If(pe.value_load(over[0:1, 0:1], min_val=0, max_val=1) > 0):
                    comb = work[:, 17, :].rearrange("p (t e) -> p t e", t=TT)
                    for t in range(TT):
                        last = tr(PS[0:NE, 1, t * P:(t + 1) * P], comb[:, t, :], tab("ident"))
                    last.then_inc(sems["tpsum"], 1)
                    pe.wait_ge(sems["t"], 1)
                    for e in range(NE):
                        if e % 2 == 0 and e >= 8:
                            pe.wait_ge(sems["b"], e // 2 - 3)
                        last = mm(PS[:, e // 2 % 4, (e % 2) * S:(e % 2 + 1) * S],
                                  tabs[0:NE, TAB["ident"]][:, e:e + 1].to_broadcast([NE, P]), combT,
                                  start=True, stop=True)
                        if e % 2:
                            last.then_inc(sems["bpsum"], 1)
                    pe.wait_ge(sems["b"], 8)

                    def body(g, s, e):
                        for f in range(ET):
                            u = 6 * s + f
                            pe.wait_ge(sems[f"full{u % SLOTS}"], g * 48 + 16 * (u // SLOTS + 1))
                            wait(pe, sems["g"], e * 4 + (f - 3))
                            w = slot(u)
                            for h in range(2):
                                for k in range(KT):
                                    last = mm(PS[:, f, h * S:(h + 1) * S], w[:, k, h * P:(h + 1) * P],
                                              H[:, k, 0:S], start=(k == 0), stop=(k == KT - 1))
                            last.then_inc(sems["unit"], 1)
                        for h in range(2):
                            u = 6 * s + 4 + h
                            pe.wait_ge(sems[f"full{u % SLOTS}"], g * 48 + 16 * (u // SLOTS + 1))
                            pe.wait_ge(sems["g"], e * 4 + (2 * h + 2))
                            for f in range(2):
                                for d in range(KT):
                                    last = mm(PS[:, 4 + d // 2, (d % 2) * S:(d % 2 + 1) * S],
                                              ring[:, u % SLOTS, f * D + d * P:f * D + (d + 1) * P],
                                              G[:, 4 * s + 2 * h + f, 0:S], start=False, stop=False,
                                              skip_group_check=True)
                            last.then_inc(sems["unit"], 1)
                    repeat(pe, NE, 2, body, peel=1)

            first_mods()
            pe.wait_ge(ld_rest, REST)
            norm(0)
            up(0)
            down(0)
            norm(1)
            mixer_a()
            norm(2)
            up(1)
            down(1)
            norm(3)
            up(2)
            down(2)
            norm(4)
            mixer_c()
            norm(5)
            up(3)
            down(3)
            norm(6)
            mixer_e()
            norm(7)
            moe(0)
            norm(8)
            mixer_o()
            norm(9)
            moe(1)

        @block.scalar
        def _(act):
            line = Line(act, act_line)
            af = act.activation

            def load_table(number):
                act.add_instruction(mybir.InstLoadActFuncSet(name=nc.get_next_instruction_name(), ins=[], outs=[],
                                                             act_func_set_id=number))

            def norm(n):
                N, base, shift, _, _, before = NORMS[n]
                load_table(SQRT)
                for d in range(KT):
                    wait(act, x_updated, UPDATES[before] - (KT - 1 - d) * (N // S) if n else 0)
                    af(squares(n, d), X[:, d, 0:N], ACT.Square).then_inc(sq_ready, 1)
                act.wait_ge(ms_psum, n + 1)
                af(rt[:, 0:N], mean_squares(n), ACT.Sqrt, bias=eps[:, 0:1]).then_inc(rt_ready, 1)
                for d in range(KT):
                    act.wait_ge(xn_ready, KT * n + d + 1)
                    for j in range(N // S):
                        h = H[:, d, j * S:(j + 1) * S]
                        af(h, h, ACT.Identity, scale=NA[:, n, j, d:d + 1],
                           bias=mod_col(base, shift, d, j)).then_inc(h_ready, 1)

            def up(f):
                N = NORMS[FFNS[f][0]][0]
                for n, stride, u0, j0, rows in ups(f):
                    def body(g, s, i):
                        act.wait_ge(unit_done, i * stride + (u0 + 1))
                        wait(act, g_ready, i + (FT * f + j0 - 3))
                        src = PS[:, 2 * (s % 2), :] if N > S else PS[:, s % 4, 0:S]
                        af(SG[:, s % 4, 0:N], src, ACT.Silu).then_inc(silu_ready, 1)
                    repeat(act, n, 4, body, peel=(1 if f == 0 else 0))

            def evacuate(name, tile, unit, dst, src_width=BANK, func=ACT.Copy):
                act.wait_ge(unit_done, UNIT0[name] + unit + 1)
                src = PS[:, tile % 4, :]
                if len(dst.shape) == 3:
                    src = src.rearrange("p (t n) -> p t n", t=dst.shape[1])
                af(dst, src, func).then_inc(lin_ready, 1)

            def head_norm(which, src, sq, r, n):
                for c in range(n):
                    w = slice(c * BANK, (c + 1) * BANK)
                    af(sq[:, w], src[:, w], ACT.Square).then_inc(hsq_ready, 1)
                for c in range(n):
                    act.wait_ge(hms_psum, HEAD0[which] + c + 1)
                    af(r[:, c * BANK:(c + 1) * BANK], PS[:, c, :], ACT.Sqrt, bias=eps[:, 0:1])\
                        .then_inc(hrt_ready, 1)

            def attention(which):
                first = 0 if which == "a" else 16
                keys, cat0 = (4, 0) if which == "a" else (2, 4)
                W = keys * P
                for s in range(19):
                    if s < 16:
                        act.wait_ge(at_max, first + s + 1)
                        if s >= 4:
                            act.wait_ge(at_tpsum, first + s - 3)
                        src = PS[:, s % 4, :] if which == "a" else PROBS[:, s % 4, 0:W]
                        af(PROBS[:, s % 4, 0:W], src, ACT.Exp, scale=(0.125 if which == "a" else 1.0),
                           bias=small[:, 4 + s % 4:5 + s % 4], accum_out=small[:, 8 + s % 4:9 + s % 4])\
                            .then_inc(at_exp, 1)
                    if 2 <= s <= 17:
                        it = s - 2
                        act.wait_ge(at_tpsum, first + it + 1)
                        if it >= 2:
                            act.wait_ge(at_out, first + it - 1)
                        af(PT[:, it % 2, 0:W], PS[:, 4 + it % 2, 0:W], ACT.Copy).then_inc(at_tready, 1)
                    if s >= 3 and (s - 3) % 4 == 3:
                        i = (s - 3) // 4
                        act.wait_ge(at_out, first + 4 * i + 4)
                        af(CAT[:, cat0 + i, :], PS[:, 6 + i % 2, 0:S], ACT.Copy).then_inc(at_kept, 1)

            def mixer_a():
                for t, u in enumerate((0, 1, 2)):
                    evacuate("a_in", t, u, A_QK[:, t * BANK:(t + 1) * BANK])
                evacuate("a_in", 3, 2, A_V[:, :, :])
                for t, u in ((4, 3), (5, 4)):
                    evacuate("a_in", t, u, A_P[:, :, (t - 4) * S:(t - 3) * S])
                act.wait_ge(lin_ready, 6)
                head_norm("a", A_QK, A_SQ, A_R, 3)
                act.wait_ge(pool_psum, 1)
                for c in range(2):
                    af(A_POOLED[:, 2 * c:2 * c + 2, :], PS[:, 4 + c, :].rearrange("p (g n) -> p g n", g=2),
                       ACT.Copy).then_inc(pool_ready, 1)
                act.wait_ge(cat_ready, 1)
                attention("a")

            def mixer_c():
                for t in range(4):
                    evacuate("c_in", t, t, C_U[:, 2 * t:2 * t + 2, :], func=ACT.Gelu_apprx_tanh)
                for t in range(4):
                    evacuate("c_in", 4 + t, 4 + t, C_V[:, :, t * S:(t + 1) * S], func=ACT.Gelu_apprx_tanh)
                act.wait_ge(lin_ready, LIN_TILE0["c_in"] + 8)
                for t in range(TT):
                    line(af(C_SQ[:, t, :], C_V[:, t, :], ACT.Square, accum_out=small[:, 16 + t:17 + t]))
                line.wait()
                af(small[:, 18:20], small[:, 16:18], ACT.Sqrt, scale=1.0 / D, bias=eps[:, 0:1]).then_inc(v_sums, 1)

            def mixer_e():
                for t in range(8):
                    evacuate("e_in", t, t, E_QK[:, t * BANK:(t + 1) * BANK])
                for t in (8, 9):
                    evacuate("e_in", t, t, E_G[:, (t - 8) * BANK:(t - 7) * BANK], func=ACT.Silu)
                for t in range(10, 14):
                    evacuate("e_in", t, t, E_V[:, :, (t - 10) * S:(t - 9) * S])
                act.wait_ge(lin_ready, LIN_TILE0["e_in"] + 14)
                act.wait_ge(rot_ready, 7)
                head_norm("e", E_QK[:, 2048:4096], E_T, E_R, 4)
                act.wait_ge(hn_ready, HEAD0["e"] + 4)
                for c in range(2):
                    act.wait_ge(re_out, 2 * c + 2)
                    af(E_T[:, c * BANK:(c + 1) * BANK], PS[:, 4 + c, :], ACT.Copy).then_inc(re_kept, 1)
                act.wait_ge(re_kept, 2)
                head_norm("r", E_T[:, 0:1024], E_T[:, 1024:2048], E_R, 2)
                act.wait_ge(cat_ready, 4)
                attention("e")

            def mixer_o():
                for t in range(8):
                    evacuate("o_in", t, t, O_QK[:, 2 * t:2 * t + 2, :])
                for t in range(8, 12):
                    evacuate("o_in", t, t, O_V[:, :, (t - 8) * S:(t - 7) * S])
                load_table(EXP_LN)
                for s in range(19):
                    if s < 16:
                        e = o_work("log", s)
                        act.wait_ge(sb_z, s + 1)
                        if s >= 2:
                            act.wait_ge(sb_l, s - 1)
                        line(af(e, o_work("z", s), ACT.Abs))
                        line.wait()
                        line(af(e, e, ACT.Exp, scale=-1.0))
                        line.wait()
                        af(e, e, ACT.Ln, bias=1.0).then_inc(sb_log, 1)
                    if 2 <= s <= 17:
                        h = s - 2
                        a = o_work("a", h)
                        act.wait_ge(sb_w, h + 1)
                        af(a, a, ACT.Exp).then_inc(sb_a, 1)
                    if s >= 3 and s % 2 == 0:
                        tile = (s - 3) // 2
                        act.wait_ge(sb_out, 2 * tile + 2)
                        af(CAT[:, tile, :], PS[:, 4 + tile % 2, 0:S], ACT.Copy).then_inc(sb_kept, 1)

            def moe(l):
                u0, e0 = UNIT0[f"moe{l}"], NE * l
                act.wait_ge(ro_psum, l + 1)
                af(work[:, 0, :], PS[:, 0, 0:TT * NE], ACT.Sigmoid).then_inc(ro_scores, 1)
                for c in range(4):
                    act.wait_ge(ht_psum, 4 * l + c + 1)
                    af(H_TOK[:, c // 2, (c % 2) * BANK:(c % 2 + 1) * BANK], PS[:, 4 + c, :], ACT.Copy)\
                        .then_inc(ht_ready, 1)

                def gathered(e, p):
                    act.wait_ge(mo_tpsum, e + (e0 + 1))
                    wait(act, mo_scattered, e + (e0 - 1))
                    af(SWT[0:CAP, p, :], PS[0:CAP, 2, 0:S], ACT.Copy).then_inc(mo_tready, 1)
                    for b in range(2):
                        act.wait_ge(mo_gpsum, e * 2 + (2 * e0 + b + 1))
                        af(HX[:, p, b * 4 * CAP:(b + 1) * 4 * CAP], PS[:, b, 0:4 * CAP], ACT.Copy)\
                            .then_inc(mo_gathered, 1)

                def body(g, s, e):
                    for f in range(ET):
                        act.wait_ge(unit_done, e * 6 + (u0 + f + 1))
                        wait(act, mo_g, e * 4 + (4 * e0 + f - 3))
                        af(SG[:, f, 0:CAP], PS[:, 2 + f % 2, 0:CAP], ACT.Silu).then_inc(mo_silu, 1)
                        if f == 1 and not (isinstance(e, int) and e == NE - 1):
                            gathered(e + 1, 1 - s)
                    act.wait_ge(unit_done, e * 6 + (u0 + 6))
                    wait(act, mo_scattered, e + e0)
                    for n in range(2):
                        af(YG[0:CAP, n * BANK:(n + 1) * BANK], PS[0:CAP, n, :], ACT.Copy).then_inc(mo_y, 1)
                gathered(0, 0)
                repeat(act, NE, 2, body, peel=1, tail=1)
                rest_pass(l)

            def rest_pass(l):
                sems = rest[l]
                with act.If(act.value_load(over[0:1, 0:1], min_val=0, max_val=1) > 0):
                    act.wait_ge(sems["tpsum"], 1)
                    af(combT, PS[0:NE, 1, 0:S], ACT.Copy).then_inc(sems["t"], 1)
                    for c in range(8):
                        act.wait_ge(sems["bpsum"], c + 1)
                        af(CB[:, 2 * c:2 * c + 2, :], PS[:, c % 4, :].rearrange("p (e n) -> p e n", e=2), ACT.Copy)\
                            .then_inc(sems["b"], 1)

                    def body(g, s, e):
                        for f in range(ET):
                            act.wait_ge(sems["unit"], e * 6 + (f + 1))
                            wait(act, sems["weighted"], e * 4 + (f - 3))
                            af(SG[:, f, 0:S], PS[:, f, 0:S], ACT.Silu).then_inc(sems["silu"], 1)
                    repeat(act, NE, 2, body, peel=1)

            act.dma_start(cols[:, :], cols_in).then_inc(ld_first, 16)
            act.dma_start(X[:, :, :], x_in).then_inc(ld_first, 16)
            for dst, src in ((tabs[:, :], tabs_in), (rel[:, :], rel_in), (router_w[:, :, :], router_in),
                             (router_b[:, :, :], router_b_in), (pool_w[:, :, :], pool_w_in),
                             (w_sp[:, :, :], w_sp_in), (b_sp[:, :, :], b_sp_in)):
                act.dma_start(dst, src).then_inc(ld_rest, 16)
            act.wait_ge(ld_first, 32)
            af(cond[:, :, :].rearrange("p k c -> p (k c)"), col("c"), ACT.Silu).then_inc(cond_ready, 1)
            c_cols = col("c").rearrange("p (k c) -> p k c", c=4)
            af(cond_rows[:, 0:N_ROWS_C, :], c_cols[:, :, 0].unsqueeze(1).to_broadcast([P, N_ROWS_C, KT]), ACT.Silu)\
                .then_inc(cond_ready, 1)
            af(cond_rows[:, N_ROWS_C:, :], c_cols[:, :, 2].unsqueeze(1).to_broadcast([P, N_ROWS - N_ROWS_C, KT]),
               ACT.Silu).then_inc(cond_ready, 1)
            act.wait_ge(eps_ready, 1)
            norm(0)
            up(0)
            norm(1)
            mixer_a()
            norm(2)
            up(1)
            norm(3)
            up(2)
            norm(4)
            mixer_c()
            norm(5)
            up(3)
            norm(6)
            mixer_e()
            norm(7)
            moe(0)
            norm(8)
            mixer_o()
            norm(9)
            moe(1)

        @block.gpsimd
        def _(pool):
            pool.memset(eps[:, :], EPS).then_inc(eps_ready, 1)
            pool.wait_ge(ext_ready, 3)
            pool.dma_start(ext_dram, ext).then_inc(ext_stored, 16)
            pool.wait_ge(ext_stored, 16)
            pool.wait_ge(acc_steps, KT * N_ROWS)
            pool.dma_start(HANKEL, bass.AP(ext_dram.tensor, 0, [[1, P], [512, 8], [1, 384]])).then_inc(ld_ext, 16)

            pool.wait_ge(ld_rest, REST)
            for h in range(16):
                z, zs, lm = (o_work(what, h) for what in ("z", "zs", "lm"))
                pool.wait_ge(sb_z, h + 1)
                if h >= 3:
                    pool.wait_ge(sb_w, h - 2)
                pool.tensor_tensor(zs, z, tab("after"), ALU.add).then_inc(sb_zs, 1)
                pool.wait_ge(sb_l, h + 1)
                pool.tensor_tensor(lm, lm, tab("before"), ALU.mult).then_inc(sb_lm, 1)

        @block.vector
        def _(dve):
            line = Line(dve, dve_line)
            tt, ts, stt = dve.tensor_tensor, dve.tensor_scalar, dve.scalar_tensor_tensor

            cond_flat = cond_rows[:, :, :].rearrange("p r k -> p (r k)")

            def take_mods(run, u):
                a, b = MOD_RUNS[run]
                dve.wait_ge(unit_done, u + 1)
                bias = cols[:, COL["mod_b"].start + a:COL["mod_b"].start + b]
                src = PS[:, 6, 2 * a:2 * b].rearrange("p (n j) -> p n j", j=2)
                line(tt(M[:, a:b, 0], src[:, :, 0], bias, ALU.add))
                tt(M[:, a:b, 1], src[:, :, 1], bias, ALU.add).then_inc(mods_ready, 1)
                dve.wait_ge(mods_ready, run + 1)
                line.wait()

            def norm_columns(n):
                N, base, _, scale, gain, _ = NORMS[n]
                g = cols[:, COL["norm"].start + gain * KT:COL["norm"].start + (gain + 1) * KT]
                for j in range(N // S):
                    at = base + scale * KT
                    line(stt(out=NA[:, n, j, :], in0=M[:, at:at + KT, j], scalar=1.0, in1=g,
                             op0=ALU.add, op1=ALU.mult))

            def norm(n):
                N = NORMS[n][0]
                norm_columns(n)
                dve.wait_ge(rt_ready, n + 1)
                line(dve.reciprocal(rs[:, 0:N], rt[:, 0:N]))
                line.wait()
                for d in range(KT):
                    tt(H[:, d, 0:N], X[:, d, 0:N], rs[:, 0:N], ALU.mult).then_inc(xn_ready, 1)

            def up(f):
                N = NORMS[FFNS[f][0]][0]
                for n, stride, u0, j0, rows in ups(f):
                    def body(g, s, i):
                        row0 = g * rows + (ROW0[f] if f < 3 else 0)
                        if rows == 3 and s >= 2:
                            take_row(row0 + (s - 2), (4, 5, 7)[s - 2])
                        dve.wait_ge(silu_ready, i + (FT * f + j0 + 1))
                        src = PS[:, 2 * (s % 2) + 1, :] if N > S else PS[:, s % 4, S:2 * S]
                        tt(row(G[:, :, 0:N], i + j0), SG[:, s % 4, 0:N], src, ALU.mult).then_inc(g_ready, 1)
                        for r, k in chunks(rows, s):
                            row_chunk(row0 + r, k, r if rows == 3 else 0, row0 + r - (2 if rows == 3 else 0))
                        if rows == 3 and s == 3:
                            take_row(row0 + 2, 7)
                        if rows == 1 and s == 3:
                            take_row(row0, 4)
                    repeat(dve, n, 4, body, peel=(1 if f == 0 else 0))

            def row_chunk(r, k, acc, summed):
                q = r * KT + k
                dve.wait_ge(rows_full[k % 4], r * 32 + 16 * (k // 4 + 1))
                w, c = ROWS_W[:, k % 4, :], cond_flat[:, bass.ds(q, 1)]
                if k == 0:
                    wait(dve, colsum_done, summed)
                    ts(ACC[acc], w, c, None, ALU.mult).then_inc(acc_steps, 1)
                else:
                    dve.wait_ge(acc_steps, q)
                    stt(out=ACC[acc], in0=w, scalar=c, in1=ACC[acc], op0=ALU.mult, op1=ALU.add)\
                        .then_inc(acc_steps, 1)

            def take_row(r, bank):
                dve.wait_ge(colsum_done, r + 1)
                tt(M[:, bass.ds(r * KT + ROW_TILE0, KT), 0:1].rearrange("p n j -> p (n j)"), PS[:, bank, 0:KT],
                   cols[:, bass.ds(r * KT + (COL["mod_b"].start + ROW_TILE0), KT)], ALU.add)\
                    .then_inc(rows_taken, 1)

            def down(f):
                N = NORMS[FFNS[f][0]][0]
                _, base, gate = FFNS[f]
                u0 = UNIT0[f"down{f}"]
                at = base + gate * KT
                for j in range(N // S):
                    line(ts(HG[:, (2 * f + j) * KT:(2 * f + j + 1) * KT], M[:, at:at + KT, j], 0.5, None, ALU.mult))
                line.wait()

                def body(g, s, i):
                    dve.wait_ge(unit_done, i + (u0 + 1))
                    for j in range(N // S):
                        x = X[:, bass.ds(i, 1), j * S:(j + 1) * S].rearrange("p a n -> p (a n)")
                        stt(out=x, in0=PS[:, s, j * S:(j + 1) * S], scalar=HG[:, bass.ds(i + (2 * f + j) * KT, 1)],
                            in1=x, op0=ALU.mult, op1=ALU.add).then_inc(x_updated, 1)
                repeat(dve, KT, SLOTS, body)

            def add_out(name, base, gate):
                for d in range(KT):
                    if d % 2 == 0:
                        dve.wait_ge(unit_done, UNIT0[name] + d // 2 + 1)
                    stt(out=X[:, d, 0:S], in0=PS[:, d // 2, (d % 2) * S:(d % 2 + 1) * S],
                        scalar=mod_col(base, gate, d, 0), in1=X[:, d, 0:S], op0=ALU.mult, op1=ALU.add)\
                        .then_inc(x_updated, 1)

            def head_norm(which, src, r, gains):
                for c, gain in enumerate(gains):
                    w = slice(c * BANK, (c + 1) * BANK)
                    dve.wait_ge(hrt_ready, HEAD0[which] + c + 1)
                    line(dve.reciprocal(r[:, w], r[:, w]))
                    line.wait()
                    if gain is None:
                        tt(src[:, w], src[:, w], r[:, w], ALU.mult).then_inc(hn_ready, 1)
                    else:
                        stt(out=src[:, w], in0=src[:, w], scalar=gain, in1=r[:, w], op0=ALU.mult, op1=ALU.mult)\
                            .then_inc(hn_ready, 1)

            def rotation(which, src, width, t, r, cos, sin):
                for c in range(0, width, BANK):
                    n = min(BANK, width - c)
                    tiles = lambda ap: ap[:, c:c + n].rearrange("p (a n) -> p a n", n=S)
                    wide = lambda name: tab(name).unsqueeze(1).to_broadcast([P, n // S, S])
                    line(tt(tiles(t), tiles(src), wide(cos), ALU.mult))
                    dve.wait_ge(rot_psum, ROT0[which] + c // BANK + 1)
                    line(tt(tiles(r), PS[:, c // BANK, 0:n].rearrange("p (a n) -> p a n", n=S), wide(sin), ALU.mult))
                    line.wait()
                    tt(src[:, c:c + n], t[:, c:c + n], r[:, c:c + n], ALU.add).then_inc(rot_ready, 1)

            def attention(which):
                first = 0 if which == "a" else 16
                W = 4 * P if which == "a" else 2 * P
                for s in range(17):
                    if s < 16:
                        top, neg = small[:, s % 4:s % 4 + 1], small[:, 4 + s % 4:5 + s % 4]
                        dve.wait_ge(at_scores, first + s + 1)
                        scores = PS[:, s % 4, 0:W]
                        if which == "e":
                            if s >= 4:
                                dve.wait_ge(at_tpsum, first + s - 3)
                            line(tt(PROBS[:, s % 4, 0:W], scores,
                                    tab("band").rearrange("p (t n) -> p t n", t=TT)[:, s % 2, :], ALU.add))
                            line.wait()
                            scores = PROBS[:, s % 4, 0:W]
                        line(dve.tensor_reduce(top, scores, AX.X, ALU.max))
                        line.wait()
                        ts(neg, top, -0.125 if which == "a" else -1.0, None, ALU.mult).then_inc(at_max, 1)
                    if s >= 1:
                        it = s - 1
                        dve.wait_ge(at_exp, first + it + 1)
                        line(dve.reciprocal(small[:, 12 + it % 4:13 + it % 4], small[:, 8 + it % 4:9 + it % 4]))
                        line.wait()
                        ts(PROBS[:, it % 4, 0:W], PROBS[:, it % 4, 0:W], small[:, 12 + it % 4:13 + it % 4], None,
                           ALU.mult).then_inc(at_probs, 1)

            def mixer_a():
                head_norm("a", A_QK, A_R, (col("q_gain"), col("q_gain"), col("k_gain")))
                dve.wait_ge(hn_ready, 3)
                dve.wait_ge(poolw_psum, 1)
                for g in range(4):
                    last = ts(CAT[:, 4 + g, :], PS[:, 6 + g // 2, (g % 2) * S:(g % 2 + 1) * S],
                              cols[:, COL["pool_scale"].start + g:COL["pool_scale"].start + g + 1], None, ALU.mult)
                last.then_inc(cat_ready, 1)
                rotation("a", A_QK, 5 * S, A_SQ, A_R, "cos_axial", "sin_axial")
                attention("a")
                add_out("a_out", 0, 5)

            def mixer_c():
                dve.wait_ge(v_sums, 1)
                line(dve.reciprocal(small[:, 20:22], small[:, 18:20]))
                line.wait()
                for t in range(TT):
                    ts(C_V[:, t, :], C_V[:, t, :], small[:, 20 + t:21 + t], None, ALU.mult).then_inc(v_ready, 1)
                for g in range(8):
                    if g % 2 == 0:
                        dve.wait_ge(sv_psum, g // 2 + 1)
                    src = PS[:, 4 + g // 2, (g % 2) * S:(g % 2 + 1) * S].rearrange("p (t n) -> p t n", t=TT)
                    line(stt(out=C_T[:, g, :].rearrange("p (t n) -> p t n", t=TT), in0=src,
                             scalar=cols[:, COL["v_gain"].start + g:COL["v_gain"].start + g + 1],
                             in1=b_sp[:, g, :].unsqueeze(1).to_broadcast([P, TT, P]), op0=ALU.mult, op1=ALU.add))
                line.wait()
                dve.tensor_tensor(CAT[:, :, :], C_T[:, :, :], C_U[:, :, :], ALU.mult).then_inc(cat_ready, 1)
                add_out("c_out", 72, 5)

            def mixer_e():
                line(ts(small[:, 24:25], col("aq_gain"), 0.125, None, ALU.mult))
                dve.wait_ge(lin_ready, LIN_TILE0["e_in"] + 4)
                rotation("e", E_QK, 2048, E_T, E_R, "cos_half", "sin_half")
                head_norm("e", E_QK[:, 2048:4096], E_R, (small[:, 24:25],) * 2 + (col("ak_gain"),) * 2)
                for h in range(4):
                    dve.wait_ge(re_scores, h + 1)
                    tt(SG[:, h, :], PS[:, h, :], tab("decay")[:, h * BANK:(h + 1) * BANK], ALU.mult)\
                        .then_inc(re_decayed, 1)
                head_norm("r", E_T[:, 0:1024], E_R, (None, None))
                dve.wait_ge(hn_ready, HEAD0["r"] + 2)
                for c in range(2):
                    w = slice(c * BANK, (c + 1) * BANK)
                    tt(CAT[:, 2 * c:2 * c + 2, :].rearrange("p a n -> p (a n)"), E_T[:, w], E_G[:, w], ALU.mult)\
                        .then_inc(cat_ready, 1)
                dve.wait_ge(cat_ready, 4)
                attention("e")
                add_out("e_out", 144, 2)

            def mixer_o():
                for s in range(18):
                    if s < 16:
                        z = o_work("z", s)
                        dve.wait_ge(sb_scores, s + 1)
                        if s >= 2:
                            dve.wait_ge(sb_zs, s - 1)
                        ts(z, PS[:, s % 2, 0:384], 0.125, None, ALU.mult).then_inc(sb_z, 1)
                    if s >= 2:
                        h = s - 2
                        dve.wait_ge(sb_sums, h + 1)
                        if h >= 2:
                            dve.wait_ge(sb_out, h - 1)
                        tt(o_work("a", h), o_work("zs", h), PS[:, 2 + h % 2, 0:384], ALU.subtract).then_inc(sb_w, 1)
                    if s < 16:
                        dve.wait_ge(sb_log, s + 1)
                        dve.wait_ge(sb_z, s + 1)
                        stt(out=o_work("lm", s), in0=z, scalar=0.0, in1=o_work("log", s), op0=ALU.max, op1=ALU.add)\
                            .then_inc(sb_l, 1)
                add_out("o_out", 192, 2)

            def route(l):
                w = lambda i: work[:, i, :]
                w8 = lambda i: work[:, i, 0:8]
                w2 = lambda i: work[:, i, 0:2]
                by_token = lambda ap: ap.rearrange("p (t e) -> p t e", t=TT)
                by_group = lambda ap: ap.rearrange("p (g e) -> p g e", e=4)
                per_token = lambda i, n: w2(i).unsqueeze(2).to_broadcast([P, TT, n])
                per_group = lambda i: w8(i).unsqueeze(2).to_broadcast([P, 8, 4])

                def step(instruction):
                    line(instruction)
                    line.wait()

                def first_best(dst, value, best, key, weights, n):
                    step(dve.tensor_reduce(w2(best), by_token(value), AX.X, ALU.max))
                    step(tt(by_token(key), by_token(value), per_token(best, n), ALU.is_equal))
                    step(tt(key, key, weights, ALU.mult))
                    step(dve.tensor_reduce(w2(best), by_token(key), AX.X, ALU.max))
                    step(tt(by_token(dst), by_token(key), per_token(best, n), ALU.is_equal))

                dve.wait_ge(ro_scores, l + 1)
                step(tt(w(1), w(0), router_b[:, :, :].rearrange("p t e -> p (t e)"), ALU.add))
                e = [by_group(w(1))[:, :, i] for i in range(4)]
                line(tt(w8(2), e[0], e[1], ALU.max))
                line(tt(w8(3), e[0], e[1], ALU.min))
                line(tt(w8(4), e[2], e[3], ALU.max))
                step(tt(w8(5), e[2], e[3], ALU.min))
                line(tt(w8(6), w8(2), w8(4), ALU.max))
                line(tt(w8(7), w8(2), w8(4), ALU.min))
                step(tt(w8(8), w8(3), w8(5), ALU.max))
                step(tt(w8(9), w8(7), w8(8), ALU.max))
                step(tt(w8(10), w8(6), w8(9), ALU.add))
                first_best(w8(11), w8(10), 12, w8(13), tab("w4"), 4)
                line(ts(w8(14), w8(11), BIG, -BIG, ALU.mult, ALU.add))
                step(tt(by_group(w(15)), by_group(w(1)), per_group(11), ALU.mult))
                step(tt(by_group(w(15)), by_group(w(15)), per_group(14), ALU.add))
                first_best(w(16), w(15), 12, w(17), tab("w16"), NE)
                step(stt(out=w(15), in0=w(16), scalar=-2.0 * BIG, in1=w(15), op0=ALU.mult, op1=ALU.add))
                first_best(w(18), w(15), 12, w(17), tab("w16"), NE)
                tt(w(16), w(16), w(18), ALU.add).then_inc(ro_masks, 1)
                dve.wait_ge(ro_masks, l + 1)
                step(tt(w(19), w(0), w(16), ALU.mult))
                step(dve.tensor_reduce(w2(20), by_token(w(19)), AX.X, ALU.add))
                step(dve.reciprocal(w2(21), w2(20)))
                line(tt(by_token(w(22)), by_token(w(19)), per_token(21, NE), ALU.mult))
                dve.wait_ge(ro_ranks, l + 1)
                step(stt(out=w(23), in0=PS[:, 1, 0:2 * NE], scalar=1.0, in1=w(16), op0=ALU.add, op1=ALU.mult))
                step(ts(w(23), w(23), -1.0, None, ALU.add))
                step(dve.tensor_reduce(w2(20)[:, 0:1], PS[:, 1, 2 * NE:3 * NE], AX.X, ALU.max))
                line(ts(over[:, :], w2(20)[0:1, 0:1], CAP + 0.5, None, ALU.is_gt))
                step(ts(w(17), w(23), CAP - 0.5, None, ALU.is_gt))
                tt(w(17), w(17), w(22), ALU.mult).then_inc(ro_listed, 1)

            def moe(l):
                u0, e0 = UNIT0[f"moe{l}"], NE * l
                route(l)
                dve.wait_ge(ro_listed, l + 1)

                def lists(e, p):
                    wait(dve, mo_gpsum, e * 2 + (2 * e0 - 2))
                    for t in range(TT):
                        place, weight = (work[:, i, bass.ds(e + t * NE, 1)] for i in (23, 22))
                        ts(SELW[:, p, t, :], tab("iota"), place, weight, ALU.is_equal, ALU.mult)
                        last = ts(SEL[:, p, t, :], tab("iota"), place, None, ALU.is_equal)
                    last.then_inc(mo_sel, 1)

                def body(g, s, e):
                    for f in range(ET):
                        dve.wait_ge(mo_silu, e * 4 + (4 * e0 + f + 1))
                        if f == 0:
                            wait(dve, unit_done, e * 6 + (u0 - 6))
                        tt(GX[:, s, f, :], SG[:, f, 0:CAP], PS[:, 2 + f % 2, CAP:2 * CAP], ALU.mult).then_inc(mo_g, 1)
                        if f == 0 and not (isinstance(e, int) and e == NE - 1):
                            lists(e + 1, 1 - s)
                lists(0, 0)
                repeat(dve, NE, 2, body, peel=1, tail=1)
                rest_pass(l)
                dve.wait_ge(y_psum, l + 1)
                for d in range(KT):
                    stt(out=X[:, d, 0:S], in0=PS[:, 4 + d // 2, (d % 2) * S:(d % 2 + 1) * S],
                        scalar=mod_col(144 + 48 * l, 5, d, 0), in1=X[:, d, 0:S], op0=ALU.mult, op1=ALU.add)\
                        .then_inc(x_updated, 1)

            def rest_pass(l):
                sems = rest[l]
                with dve.If(dve.value_load(over[0:1, 0:1], min_val=0, max_val=1) > 0):
                    def body(g, s, e):
                        for f in range(ET):
                            dve.wait_ge(sems["silu"], e * 4 + (f + 1))
                            tt(SG[:, f, S:2 * S], SG[:, f, 0:S], row(CB, e), ALU.mult).then_inc(sems["weighted"], 1)
                            dve.wait_ge(sems["weighted"], e * 4 + (f + 1))
                            wait(dve, sems["unit"], e * 6 - 6)
                            tt(G[:, 4 * s + f, 0:S], SG[:, f, S:2 * S], PS[:, f, S:2 * S], ALU.mult)\
                                .then_inc(sems["g"], 1)
                    repeat(dve, NE, 2, body, peel=1)

            dve.wait_ge(ld_rest, REST)
            dve.tensor_copy(ext[:, 0:127], rel[:, 0:1].to_broadcast([8, 127])).then_inc(ext_ready, 1)
            dve.tensor_copy(ext[:, 127:319], rel[:, :]).then_inc(ext_ready, 1)
            dve.tensor_copy(ext[:, 319:512], rel[:, REL - 1:REL].to_broadcast([8, 193])).then_inc(ext_ready, 1)
            dve.wait_ge(ld_first, 32)
            take_mods(0, UNIT0["mod"] + 11)
            dve.wait_ge(cond_ready, 3)
            dve.wait_ge(ext_stored, 16)
            norm(0)
            up(0)
            take_mods(1, UNIT0["down0"] - 1)
            down(0)
            norm(1)
            mixer_a()
            norm(2)
            up(1)
            down(1)
            norm(3)
            up(2)
            down(2)
            norm(4)
            mixer_c()
            norm(5)
            up(3)
            down(3)
            norm(6)
            mixer_e()
            norm(7)
            moe(0)
            norm(8)
            mixer_o()
            norm(9)
            moe(1)


def units_of(w):
    m = w.shape[-1]
    return w.reshape(KT, P, m // 256, 256).transpose(2, 1, 0, 3).reshape(m // 256, P, UW)


def pairs_of(gate, up):
    m = gate.shape[-1]
    both = np.stack([gate, up], 1).reshape(KT, P, 2, m // P, P)
    return both.transpose(3, 1, 0, 2, 4).reshape(m // P, P, UW)


def by_partition(v):
    return v.reshape(-1, P).T


def kernel(**inputs):
    import concourse.bacc as bacc
    from concourse.bass_utils import run_bass_kernel_spmd

    a = {k: np.ascontiguousarray(v) for k, v in inputs.items()}
    x_in = np.concatenate([a["x"][0], a["ctx"][0]], 0).T.reshape(KT, P, 2 * S).transpose(1, 0, 2)
    c = [by_partition(v) for v in (a["c"][0], a["c_ctx"], a["c_2"][0], a["c_2"][0])]
    cols = np.concatenate([
        np.stack(c, 2).reshape(P, -1),
        by_partition(np.concatenate([a["b_mod"].reshape(-1), a["ada_b_2"].reshape(-1)])),
        by_partition(np.concatenate([a["norm_g"].reshape(-1), a["norm1_g_2"].reshape(-1), a["norm2_g_2"].reshape(-1)])),
        by_partition(a["pool_scale"][0]), by_partition(a["v_norm_g"][0]),
        *(np.tile(v, 2)[:, None] for v in (a["qk_norm_g"][0, 0], a["qk_norm_g"][0, 1],
                                           a["att_q_norm_g_2"][0], a["att_k_norm_g_2"][0]))], 1)
    heads = np.concatenate([np.arange(h * 64, h * 64 + 64) for i in range(4) for h in (i, 4 + i)])
    w_in_a = a["w_in_a"][0]
    w_in_a = np.concatenate([w_in_a[:, heads], w_in_a[:, 512:]], 1)
    w_out_a = a["w_out_a"][0]
    w_out_a = np.concatenate([w_out_a[heads], w_out_a[512:]], 0)
    even = np.split(a["even_w_in_2"][0], 7, axis=1)
    even = np.concatenate([even[i] for i in (0, 1, 4, 5, 3, 2, 6)], 1)
    lin = np.concatenate([units_of(w) for w in (w_in_a, w_out_a, a["w_in_c"][0], a["w_out_c"][0], even,
                                                a["even_w_out_2"][0], a["odd_w_in_2"][0], a["odd_w_out_2"][0])])
    mod = units_of(a["w_mod"][0][:, :5 * D])
    mod_rows = np.concatenate([w.reshape(KT, P, -1, D).transpose(2, 0, 1, 3).reshape(-1, P, D)
                               for w in (a["w_mod"][0][:, 5 * D:], a["w_mod"][1], *a["ada_w_2"])])
    w13 = a["ffn_w13"].reshape(4, D, 2 * FF)
    up = np.concatenate([pairs_of(w[:, :FF], w[:, FF:]) for w in w13])
    w2 = a["ffn_w2"].reshape(4, FT, P, KT, P)
    down = w2.transpose(0, 3, 2, 1, 4).reshape(4 * KT, P, FT * P)
    moe = np.empty((2, NE, 6, P, UW), np.float32)
    for l in range(2):
        for e in range(NE):
            moe[l, e, 0:4] = pairs_of(a["exp_w_gate_2"][l, e], a["exp_w_up_2"][l, e])
            moe[l, e, 4:6] = a["exp_w_down_2"][l, e].reshape(2, 2, P, D).transpose(0, 2, 1, 3).reshape(2, P, UW)
    arrays = {
        "x_in": x_in, "cols_in": cols, "tabs_in": tables(),
        "pool_w_in": a["pool_w"][0].transpose(1, 0, 2), "w_sp_in": a["w_sp"][0].transpose(2, 0, 1),
        "b_sp_in": np.broadcast_to(a["b_sp"][0][None], (P, 8, P)),
        "router_in": a["router_w_2"].reshape(KT, P, NE).transpose(1, 0, 2),
        "router_b_in": np.broadcast_to(a["router_b_2"], (P, TT, NE)),
        "rel_in": a["att_rel_bias_2"][0][:, ::-1],
        "mod_w": mod, "mod_rows": mod_rows, "up_w": up, "down_w": down, "lin_w": lin, "moe_w": moe.reshape(-1, P, UW),
    }
    arrays = {k: np.ascontiguousarray(v) for k, v in arrays.items()}
    nc = bacc.Bacc("TRN2", target_bir_lowering=False, num_devices=1)
    aps = {k: nc.dram_tensor(k, v.shape, F32, kind="ExternalInput").ap() for k, v in arrays.items()}
    ext_dram = nc.dram_tensor("ext_dram", (8, 512), F32, kind="Internal").ap()
    out = nc.dram_tensor("out", (P, KT, S), F32, kind="ExternalOutput").ap()
    program(nc, ext_dram=ext_dram, out=out, **aps)
    got = run_bass_kernel_spmd(nc, [arrays], core_ids=[0]).results[0]["out"]
    return got.transpose(2, 1, 0).reshape(1, S, D)
```
